# Optimizing a Trainium2 kernel written in Bass

```python
import math
import jax, jax.numpy as jnp
from jax import lax
import numpy as np

D_MODEL = 1024
BATCH = 1
SEQ = 512
DEPTH = 1

D_BRANCH = 512
N_BRANCHES = 3
EPS = 1e-6
GMLP_CHUNK = 128
GMLP_GROUPS = 4
GMLP_GDIM = D_BRANCH // GMLP_GROUPS
GLA_HEADS = 4
GLA_DK = D_BRANCH // 2 // GLA_HEADS
GLA_DV = D_BRANCH // GLA_HEADS
GLA_GATE_RANK = 16
GLA_GATE_TAU = 16.0
GLA_CHUNK = 64
DSA_HEADS = 4
DSA_HDIM = D_BRANCH // DSA_HEADS
DSA_IDX_HEADS = 4
DSA_IDX_DIM = 64
DSA_QBLOCK = 128
DSA_TOPK_MAX = 256
N_BUCKETS = 32
MAX_DISTANCE = 128
N_GROUPS = 4
EXPERTS_PER_GROUP = 4
N_EXPERTS = N_GROUPS * EXPERTS_PER_GROUP
D_EXPERT = 256
TOPK_IN_GROUP = 2

IN_SIZES = (
    D_BRANCH, D_BRANCH,
    GLA_HEADS * GLA_DK, GLA_HEADS * GLA_DK,
    GLA_HEADS * GLA_DV, GLA_HEADS * GLA_DV,
    GLA_GATE_RANK,
    DSA_HEADS * DSA_HDIM, DSA_HEADS * DSA_HDIM, DSA_HEADS * DSA_HDIM,
    DSA_IDX_HEADS * DSA_IDX_DIM, DSA_IDX_DIM, DSA_IDX_HEADS,
    N_BRANCHES * D_MODEL,
)
N_IN = sum(IN_SIZES)


def rms_norm(x, g):
    xf = x.astype(jnp.float32)
    y = xf * lax.rsqrt(jnp.mean(xf * xf, axis=-1, keepdims=True) + EPS)
    return (y * g.astype(jnp.float32)).astype(x.dtype)

def layer_norm(x, g, b):
    xf = x.astype(jnp.float32)
    mu = jnp.mean(xf, axis=-1, keepdims=True)
    var = jnp.mean(jnp.square(xf - mu), axis=-1, keepdims=True)
    y = (xf - mu) * lax.rsqrt(var + EPS)
    return (y * g.astype(jnp.float32) + b.astype(jnp.float32)).astype(x.dtype)

def t5_bucket(rel):
    n = jnp.maximum(rel, 0)
    max_exact = N_BUCKETS // 2
    large = max_exact + (
        jnp.log(jnp.maximum(n, max_exact).astype(jnp.float32) / max_exact)
        / math.log(MAX_DISTANCE / max_exact) * (N_BUCKETS - max_exact)
    ).astype(jnp.int32)
    large = jnp.minimum(large, N_BUCKETS - 1)
    return jnp.where(n < max_exact, n, large)

def gmlp_branch(u, v, ln_g, ln_b, w_s, b_s):
    bsz, s, _ = v.shape
    v = layer_norm(v, ln_g, ln_b)
    vc = v.reshape(bsz, s // GMLP_CHUNK, GMLP_CHUNK, GMLP_GROUPS, GMLP_GDIM)
    causal = jnp.tril(jnp.ones((GMLP_CHUNK, GMLP_CHUNK), dtype=bool))
    w = jnp.where(causal[None], w_s, jnp.zeros_like(w_s))
    mixed = jnp.einsum('gts,bcsgd->bctgd', w, vc) + b_s.T[:, :, None]
    return u * mixed.reshape(bsz, s, D_BRANCH)

def gla_scan(q, k, v, g):
    bsz, s, h, _ = q.shape
    out_dtype = v.dtype
    q = q.astype(jnp.float32) * (GLA_DK ** -0.5)

    def to_chunks(t):
        t = t.astype(jnp.float32)
        return t.reshape(bsz, s // GLA_CHUNK, GLA_CHUNK, h, t.shape[-1]).transpose(1, 0, 3, 2, 4)

    causal = jnp.tril(jnp.ones((GLA_CHUNK, GLA_CHUNK), dtype=bool))[None, None, :, :, None]

    def step(state, inp):
        qc, kc, vc, gc = inp
        b = jnp.cumsum(gc, axis=2)
        b_last = b[:, :, -1:, :]
        o_inter = jnp.einsum('bhtd,bhde->bhte', qc * jnp.exp(b), state)
        diff = b[:, :, :, None, :] - b[:, :, None, :, :]
        decay = jnp.where(causal, jnp.exp(jnp.minimum(diff, 0.0)), 0.0)
        attn = jnp.einsum('bhtd,bhsd,bhtsd->bhts', qc, kc, decay)
        o = o_inter + jnp.einsum('bhts,bhse->bhte', attn, vc)
        new_state = (jnp.exp(b_last[:, :, 0, :])[..., None] * state
                     + jnp.einsum('bhsd,bhse->bhde', kc * jnp.exp(b_last - b), vc))
        return new_state, o

    state0 = jnp.zeros((bsz, h, GLA_DK, GLA_DV), jnp.float32)
    _, o = lax.scan(step, state0, (to_chunks(q), to_chunks(k), to_chunks(v), to_chunks(g)))
    return o.transpose(1, 0, 3, 2, 4).reshape(bsz, s, h, GLA_DV).astype(out_dtype)

def dsa_attention(q, k, v, iq, ik, iw, rel_bias):
    bsz, s, h, hd = q.shape
    n_blocks = s // DSA_QBLOCK
    topk = min(DSA_TOPK_MAX, s // 4)
    key_pos = jnp.arange(s, dtype=jnp.int32)
    gather = jax.vmap(lambda arr, idx: arr[idx])

    def block(i):
        start = i * DSA_QBLOCK
        qb = lax.dynamic_slice_in_dim(q, start, DSA_QBLOCK, axis=1)
        iqb = lax.dynamic_slice_in_dim(iq, start, DSA_QBLOCK, axis=1)
        iwb = lax.dynamic_slice_in_dim(iw, start, DSA_QBLOCK, axis=1)
        qpos = start + jnp.arange(DSA_QBLOCK, dtype=jnp.int32)
        raw = jnp.einsum('bthd,bsd->bths', iqb, ik)
        score = jnp.einsum('bths,bth->bts', jax.nn.relu(raw), iwb).astype(jnp.float32)
        admissible = key_pos[None, :] <= qpos[:, None]
        score = jnp.where(admissible[None], score, -jnp.inf)
        _, top_idx = lax.top_k(score, topk)
        valid = top_idx <= qpos[None, :, None]
        kg = gather(k, top_idx)
        vg = gather(v, top_idx)
        logits = jnp.einsum('bthd,btkhd->btkh', qb, kg).astype(jnp.float32) * (hd ** -0.5)
        bias = rel_bias[t5_bucket(qpos[None, :, None] - top_idx)].astype(jnp.float32)
        logits = jnp.where(valid[..., None], logits + bias, -1e30)
        p = jax.nn.softmax(logits, axis=2).astype(v.dtype)
        return jnp.einsum('btkh,btkhd->bthd', p, vg)

    out = lax.map(block, jnp.arange(n_blocks))
    return out.transpose(1, 0, 2, 3, 4).reshape(bsz, s, h * hd)

def hybrid_mixer(h, w_in, gmlp_ln_g, gmlp_ln_b, gmlp_w_s, gmlp_b_s, gla_w_gate2, gla_b_gate,
                 gla_norm_g, dsa_qnorm_g, dsa_knorm_g, rel_bias, w_branch, b_branch_gate, w_out):
    bsz, s, _ = h.shape
    proj = h @ w_in
    splits = np.cumsum(IN_SIZES)[:-1].tolist()
    (a_u, a_v, g_q, g_k, g_v, g_r, g_a, d_q, d_k, d_v, d_iq, d_ik, d_iw, gates) = jnp.split(
        proj, splits, axis=-1)

    y_a = gmlp_branch(jax.nn.gelu(a_u), jax.nn.gelu(a_v), gmlp_ln_g, gmlp_ln_b, gmlp_w_s, gmlp_b_s)

    log_alpha = jax.nn.log_sigmoid((g_a @ gla_w_gate2 + gla_b_gate).astype(jnp.float32)) / GLA_GATE_TAU
    o_b = gla_scan(g_q.reshape(bsz, s, GLA_HEADS, GLA_DK), g_k.reshape(bsz, s, GLA_HEADS, GLA_DK),
                   g_v.reshape(bsz, s, GLA_HEADS, GLA_DV),
                   log_alpha.reshape(bsz, s, GLA_HEADS, GLA_DK))
    o_b = rms_norm(o_b, gla_norm_g) * jax.nn.silu(g_r.reshape(bsz, s, GLA_HEADS, GLA_DV))
    y_b = o_b.reshape(bsz, s, D_BRANCH)

    q = rms_norm(d_q.reshape(bsz, s, DSA_HEADS, DSA_HDIM), dsa_qnorm_g)
    k = rms_norm(d_k.reshape(bsz, s, DSA_HEADS, DSA_HDIM), dsa_knorm_g)
    y_c = dsa_attention(q, k, d_v.reshape(bsz, s, DSA_HEADS, DSA_HDIM),
                        d_iq.reshape(bsz, s, DSA_IDX_HEADS, DSA_IDX_DIM), d_ik, d_iw, rel_bias)

    ys = jnp.stack([y_a, y_b.astype(y_a.dtype), y_c.astype(y_a.dtype)], axis=0)
    up = jnp.einsum('nbse,ned->bsnd', ys, w_branch)
    gate = jax.nn.sigmoid(gates.reshape(bsz, s, N_BRANCHES, D_MODEL) + b_branch_gate)
    merged = jnp.sum(gate * up, axis=2)
    return (merged @ w_out).astype(h.dtype)

def hier_moe(h, w_group, b_group, w_router, b_router, w_exp_gate, w_exp_up, w_exp_down):
    bsz, s, d = h.shape
    hf = h.reshape(-1, d)
    grp_prob = jax.nn.softmax((hf @ w_group + b_group).astype(jnp.float32), axis=-1)
    p_g, g_idx = lax.top_k(grp_prob, 1)
    g_onehot = jax.nn.one_hot(g_idx[:, 0], N_GROUPS, dtype=jnp.float32)
    exp_logits = (hf @ w_router + b_router).astype(jnp.float32).reshape(-1, N_GROUPS, EXPERTS_PER_GROUP)
    sel_logits = jnp.einsum('tge,tg->te', exp_logits, g_onehot)
    top_vals, e_idx = lax.top_k(sel_logits, TOPK_IN_GROUP)
    weights = p_g * jax.nn.softmax(top_vals, axis=-1)
    eid = g_idx * EXPERTS_PER_GROUP + e_idx
    combine = jnp.einsum('tk,tke->te', weights,
                         jax.nn.one_hot(eid, N_EXPERTS, dtype=jnp.float32)).astype(hf.dtype)
    y = jnp.zeros_like(hf)
    for gi in range(N_GROUPS):
        sl = slice(gi * EXPERTS_PER_GROUP, (gi + 1) * EXPERTS_PER_GROUP)
        hg = jnp.einsum('td,edf->etf', hf, w_exp_gate[sl])
        hu = jnp.einsum('td,edf->etf', hf, w_exp_up[sl])
        act = jax.nn.silu(hg) * hu * combine[:, sl].T[:, :, None]
        y = y + jnp.einsum('etf,efd->td', act, w_exp_down[sl]).astype(hf.dtype)
    return y.reshape(bsz, s, d)

def first_inputs(seed: int = 0) -> dict:
    key = jax.random.key(seed)
    ks = jax.random.split(key, 28)
    L = DEPTH

    def nrm(k, shape, scale):
        return jax.random.normal(k, shape, jnp.float32) * scale

    return {
        "x": nrm(ks[0], (BATCH, SEQ, D_MODEL), 1.0),
        "c": nrm(ks[1], (BATCH, D_MODEL), 1.0),
        "w_mod": nrm(ks[2], (L, D_MODEL, 6 * D_MODEL), 0.5 * D_MODEL ** -0.5),
        "b_mod": nrm(ks[3], (L, 6 * D_MODEL), 0.02),
        "g_norm1": 1.0 + nrm(ks[4], (L, D_MODEL), 0.1),
        "g_norm2": 1.0 + nrm(ks[5], (L, D_MODEL), 0.1),
        "w_in": nrm(ks[6], (L, D_MODEL, N_IN), D_MODEL ** -0.5),
        "gmlp_ln_g": 1.0 + nrm(ks[7], (L, D_BRANCH), 0.1),
        "gmlp_ln_b": nrm(ks[8], (L, D_BRANCH), 0.02),
        "gmlp_w_s": nrm(ks[9], (L, GMLP_GROUPS, GMLP_CHUNK, GMLP_CHUNK), GMLP_CHUNK ** -0.5),
        "gmlp_b_s": 1.0 + nrm(ks[10], (L, GMLP_GROUPS, GMLP_CHUNK), 0.1),
        "gla_w_gate2": nrm(ks[11], (L, GLA_GATE_RANK, GLA_HEADS * GLA_DK), GLA_GATE_RANK ** -0.5),
        "gla_b_gate": nrm(ks[12], (L, GLA_HEADS * GLA_DK), 0.1),
        "gla_norm_g": 1.0 + nrm(ks[13], (L, GLA_DV), 0.1),
        "dsa_qnorm_g": 1.0 + nrm(ks[14], (L, DSA_HDIM), 0.1),
        "dsa_knorm_g": 1.0 + nrm(ks[15], (L, DSA_HDIM), 0.1),
        "rel_bias": nrm(ks[16], (N_BUCKETS, DSA_HEADS), 0.5),
        "w_branch": nrm(ks[17], (L, N_BRANCHES, D_BRANCH, D_MODEL), D_BRANCH ** -0.5),
        "b_branch_gate": nrm(ks[18], (L, N_BRANCHES, D_MODEL), 0.1),
        "w_out": nrm(ks[19], (L, D_MODEL, D_MODEL), D_MODEL ** -0.5),
        "w_group": nrm(ks[20], (L, D_MODEL, N_GROUPS), D_MODEL ** -0.5),
        "b_group": nrm(ks[21], (L, N_GROUPS), 0.01),
        "w_router": nrm(ks[22], (L, D_MODEL, N_EXPERTS), D_MODEL ** -0.5),
        "b_router": nrm(ks[23], (L, N_EXPERTS), 0.01),
        "w_exp_gate": nrm(ks[24], (L, N_EXPERTS, D_MODEL, D_EXPERT), D_MODEL ** -0.5),
        "w_exp_up": nrm(ks[25], (L, N_EXPERTS, D_MODEL, D_EXPERT), D_MODEL ** -0.5),
        "w_exp_down": nrm(ks[26], (L, N_EXPERTS, D_EXPERT, D_MODEL), D_EXPERT ** -0.5),
    }

def first_block(x, c, w_mod, b_mod, g_norm1, g_norm2, w_in, gmlp_ln_g, gmlp_ln_b, gmlp_w_s, gmlp_b_s,
              gla_w_gate2, gla_b_gate, gla_norm_g, dsa_qnorm_g, dsa_knorm_g, rel_bias, w_branch,
              b_branch_gate, w_out, w_group, b_group, w_router, b_router, w_exp_gate, w_exp_up,
              w_exp_down):
    c_act = jax.nn.silu(c)
    for l in range(DEPTH):
        mod = c_act @ w_mod[l] + b_mod[l]
        sh1, sc1, gt1, sh2, sc2, gt2 = [m[:, None, :] for m in jnp.split(mod, 6, axis=-1)]
        h = rms_norm(x, g_norm1[l]) * (1.0 + sc1) + sh1
        mix = hybrid_mixer(h, w_in[l], gmlp_ln_g[l], gmlp_ln_b[l], gmlp_w_s[l], gmlp_b_s[l],
                           gla_w_gate2[l], gla_b_gate[l], gla_norm_g[l], dsa_qnorm_g[l],
                           dsa_knorm_g[l], rel_bias, w_branch[l], b_branch_gate[l], w_out[l])
        x = (x + gt1 * mix).astype(x.dtype)
        h2 = rms_norm(x, g_norm2[l]) * (1.0 + sc2) + sh2
        ffn = hier_moe(h2, w_group[l], b_group[l], w_router[l], b_router[l],
                       w_exp_gate[l], w_exp_up[l], w_exp_down[l])
        x = (x + gt2 * ffn).astype(x.dtype)
    return x


N_META = 16
BLOCK_Q = 128
META_PAD = BLOCK_Q - N_META
ATTN_HEADS = 8
HEAD_DIM = 64
ATTN_WIDTH = ATTN_HEADS * HEAD_DIM
CONV_GROUPS = 8
CONV_WIDTH = 512
CONV_K = 3
D_FF = 2816
NORM_EPS = 1e-6
IN_SPLITS = (ATTN_WIDTH, ATTN_WIDTH, ATTN_WIDTH, ATTN_HEADS,
             CONV_WIDTH, CONV_WIDTH, CONV_WIDTH, D_MODEL, D_MODEL)
IN_COLS = ATTN_WIDTH * 3 + ATTN_HEADS + CONV_WIDTH * 3 + D_MODEL * 2


def rms_norm_2(x, g):
    xf = x.astype(jnp.float32)
    y = xf * lax.rsqrt(jnp.mean(xf * xf, axis=-1, keepdims=True) + NORM_EPS)
    return (y * g.astype(jnp.float32)).astype(x.dtype)

def swiglu(x, w_in, w_out):
    a, b = jnp.split(x @ w_in, 2, axis=-1)
    return (jax.nn.silu(a) * b) @ w_out

def split_cols(z):
    idx, acc = [], 0
    for s in IN_SPLITS[:-1]:
        acc += s
        idx.append(acc)
    return jnp.split(z, idx, axis=-1)

def forgetting_attention(q, k, v, log_f):
    B, L, H, Dh = q.shape
    F = jnp.cumsum(log_f, axis=1)
    n_blocks = (L + META_PAD) // BLOCK_Q
    q_blocks = jnp.pad(q, ((0, 0), (META_PAD, 0), (0, 0), (0, 0)))
    q_blocks = q_blocks.reshape(B, n_blocks, BLOCK_Q, H, Dh).transpose(1, 0, 2, 3, 4)
    fq_blocks = jnp.pad(F, ((0, 0), (META_PAD, 0), (0, 0)))
    fq_blocks = fq_blocks.reshape(B, n_blocks, BLOCK_Q, H).transpose(1, 0, 3, 2)
    f_k = F.transpose(0, 2, 1)
    k_pos = jnp.arange(L)
    scale = HEAD_DIM ** -0.5

    def one_block(args):
        blk, qb, fqb = args
        q_pos = blk * BLOCK_Q + jnp.arange(BLOCK_Q) - META_PAD
        s = jnp.einsum('bqhd,bkhd->bhqk', qb, k).astype(jnp.float32) * scale
        s = s + fqb[..., None] - f_k[:, :, None, :]
        mask = k_pos[None, :] <= jnp.maximum(q_pos, 0)[:, None]
        s = jnp.where(mask[None, None], s, -jnp.inf)
        p = jax.nn.softmax(s, axis=-1).astype(v.dtype)
        return jnp.einsum('bhqk,bkhd->bqhd', p, v)

    out = lax.map(one_block, (jnp.arange(n_blocks), q_blocks, fq_blocks))
    out = out.transpose(1, 0, 2, 3, 4).reshape(B, n_blocks * BLOCK_Q, H, Dh)
    return out[:, META_PAD:]

def short_conv(u, w):
    L = u.shape[1]
    up = jnp.pad(u, ((0, 0), (CONV_K - 1, 0), (0, 0)))
    y = up[:, 0:L] * w[0]
    for j in range(1, CONV_K):
        y = y + up[:, j:j + L] * w[j]
    return y

def hybrid_layer(h, w_in, b_forget, conv_w, w_attn_branch, w_conv_branch, w_out,
                 g_ffn1_pre, g_ffn1_post, w_ffn1_in, w_ffn1_out,
                 g_mix_pre, g_mix_post, g_ffn2_pre, g_ffn2_post, w_ffn2_in, w_ffn2_out):
    B, L, _ = h.shape
    h = h + 0.5 * rms_norm_2(swiglu(rms_norm_2(h, g_ffn1_pre), w_ffn1_in, w_ffn1_out), g_ffn1_post)
    u = rms_norm_2(h, g_mix_pre)
    q, k, v, f_logit, c_b, c_c, c_in, gate_a, gate_c = split_cols(u @ w_in)
    q = q.reshape(B, L, ATTN_HEADS, HEAD_DIM)
    k = k.reshape(B, L, ATTN_HEADS, HEAD_DIM)
    v = v.reshape(B, L, ATTN_HEADS, HEAD_DIM)
    log_f = jax.nn.log_sigmoid((f_logit + b_forget).astype(jnp.float32))
    y_attn = forgetting_attention(q, k, v, log_f).reshape(B, L, ATTN_WIDTH) @ w_attn_branch
    y_conv = (c_b * short_conv(c_c * c_in, conv_w)) @ w_conv_branch
    mixed = (jax.nn.sigmoid(gate_a) * y_attn + jax.nn.sigmoid(gate_c) * y_conv) @ w_out
    h = h + rms_norm_2(mixed, g_mix_post)
    h = h + 0.5 * rms_norm_2(swiglu(rms_norm_2(h, g_ffn2_pre), w_ffn2_in, w_ffn2_out), g_ffn2_post)
    return h

def second_inputs(seed: int = 0) -> dict:
    key = jax.random.key(seed)
    ks = jax.random.split(key, 24)
    nrm = lambda k, shape, scale: jax.random.normal(k, shape, jnp.float32) * scale
    gain = lambda k: 1.0 + 0.05 * jax.random.normal(k, (DEPTH, D_MODEL), jnp.float32)
    return {
        "x": nrm(ks[0], (BATCH, SEQ, D_MODEL), 1.0),
        "meta_tokens": nrm(ks[1], (N_META, D_MODEL), 1.0),
        "w_in": nrm(ks[2], (DEPTH, D_MODEL, IN_COLS), D_MODEL ** -0.5),
        "b_forget": nrm(ks[3], (DEPTH, ATTN_HEADS), 0.1),
        "conv_w": nrm(ks[4], (DEPTH, CONV_K, CONV_WIDTH), CONV_K ** -0.5),
        "w_attn_branch": nrm(ks[5], (DEPTH, ATTN_WIDTH, D_MODEL), ATTN_WIDTH ** -0.5),
        "w_conv_branch": nrm(ks[6], (DEPTH, CONV_WIDTH, D_MODEL), CONV_WIDTH ** -0.5),
        "w_out": nrm(ks[7], (DEPTH, D_MODEL, D_MODEL), D_MODEL ** -0.5),
        "g_ffn1_pre": gain(ks[8]),
        "g_ffn1_post": gain(ks[9]),
        "w_ffn1_in": nrm(ks[10], (DEPTH, D_MODEL, 2 * D_FF), D_MODEL ** -0.5),
        "w_ffn1_out": nrm(ks[11], (DEPTH, D_FF, D_MODEL), D_FF ** -0.5),
        "g_mix_pre": gain(ks[12]),
        "g_mix_post": gain(ks[13]),
        "g_ffn2_pre": gain(ks[14]),
        "g_ffn2_post": gain(ks[15]),
        "w_ffn2_in": nrm(ks[16], (DEPTH, D_MODEL, 2 * D_FF), D_MODEL ** -0.5),
        "w_ffn2_out": nrm(ks[17], (DEPTH, D_FF, D_MODEL), D_FF ** -0.5),
    }

def second_block(x, meta_tokens, w_in, b_forget, conv_w, w_attn_branch, w_conv_branch, w_out,
              g_ffn1_pre, g_ffn1_post, w_ffn1_in, w_ffn1_out,
              g_mix_pre, g_mix_post, g_ffn2_pre, g_ffn2_post, w_ffn2_in, w_ffn2_out):
    B = x.shape[0]
    meta = jnp.broadcast_to(meta_tokens.astype(x.dtype)[None], (B, N_META, x.shape[-1]))
    h = jnp.concatenate([meta, x], axis=1)
    for l in range(DEPTH):
        h = hybrid_layer(h, w_in[l], b_forget[l], conv_w[l], w_attn_branch[l], w_conv_branch[l], w_out[l],
                         g_ffn1_pre[l], g_ffn1_post[l], w_ffn1_in[l], w_ffn1_out[l],
                         g_mix_pre[l], g_mix_post[l], g_ffn2_pre[l], g_ffn2_post[l],
                         w_ffn2_in[l], w_ffn2_out[l])
    return h[:, N_META:]


def setup_inputs(seed=0):
    out = dict(first_inputs(seed))
    for name, value in second_inputs(seed + 1).items():
        if name != "x":
            out[name + "_2"] = value
    return out


def reference(
    x, c, w_mod, b_mod, g_norm1, g_norm2, w_in, gmlp_ln_g, gmlp_ln_b, gmlp_w_s, gmlp_b_s,
    gla_w_gate2, gla_b_gate, gla_norm_g, dsa_qnorm_g, dsa_knorm_g, rel_bias, w_branch,
    b_branch_gate, w_out, w_group, b_group, w_router, b_router, w_exp_gate, w_exp_up,
    w_exp_down, meta_tokens_2, w_in_2, b_forget_2, conv_w_2, w_attn_branch_2, w_conv_branch_2,
    w_out_2, g_ffn1_pre_2, g_ffn1_post_2, w_ffn1_in_2, w_ffn1_out_2, g_mix_pre_2, g_mix_post_2,
    g_ffn2_pre_2, g_ffn2_post_2, w_ffn2_in_2, w_ffn2_out_2,
):
    x = first_block(
        x, c, w_mod, b_mod, g_norm1, g_norm2, w_in, gmlp_ln_g, gmlp_ln_b, gmlp_w_s, gmlp_b_s,
        gla_w_gate2, gla_b_gate, gla_norm_g, dsa_qnorm_g, dsa_knorm_g, rel_bias, w_branch,
        b_branch_gate, w_out, w_group, b_group, w_router, b_router, w_exp_gate, w_exp_up,
        w_exp_down,
    )
    return second_block(
        x, meta_tokens_2, w_in_2, b_forget_2, conv_w_2, w_attn_branch_2, w_conv_branch_2,
        w_out_2, g_ffn1_pre_2, g_ffn1_post_2, w_ffn1_in_2, w_ffn1_out_2, g_mix_pre_2,
        g_mix_post_2, g_ffn2_pre_2, g_ffn2_post_2, w_ffn2_in_2, w_ffn2_out_2,
    )


_drawn_inputs = setup_inputs


def setup_inputs(seed=0):
    import zlib

    import numpy as np

    out = dict(_drawn_inputs(seed))
    spreads = {}
    factors = {'gmlp_ln_g': 4.503,
     'gmlp_ln_b': 22.964,
     'gmlp_b_s': 2.959,
     'gla_b_gate': 6.052,
     'gla_norm_g': 3.163,
     'dsa_qnorm_g': 8.0,
     'dsa_knorm_g': 8.0,
     'b_branch_gate': 4.775,
     'b_group': 51.369,
     'b_router': 44.499,
     'b_forget_2': 4.888,
     'g_ffn2_post_2': 3.684,
     'rel_bias': 4.629}
    for name, (base, spread) in spreads.items():
        noise = np.random.default_rng([zlib.crc32(name.encode()), seed]).standard_normal(out[name].shape)
        drawn = base * np.exp(spread * noise) if base else spread * noise
        out[name] = __import__('jax').numpy.asarray(drawn.astype(out[name].dtype))
    for name, factor in factors.items():
        out[name] = (out[name] * factor).astype(out[name].dtype)
    return out
```

```python
from contextlib import ExitStack

import numpy as np
import concourse.bass as bass
from concourse import mybir

F32 = mybir.dt.float32
F32R = mybir.dt.float32r
ALU = mybir.AluOpType
ACT = mybir.ActivationFunctionType
AX = mybir.AxisListType.X

P = 128
D = 1024
KT = D // P
SEQ = 512
META = 16
TALL = SEQ + META
NTOK = SEQ // P
DB = 512
BT = DB // P
EPS = 1e-6
RING = 3
CH = 2048
SLOTS = 4
TOPK = 128
REPLACED = -3.0e38
OUTSIDE = -3.3e38
BIG = 1e30
N_EXP = 16
CHUNK = 64
SUB = 16
D_FF = 2816
FF_UNITS = D_FF // 256

(A_U, A_V, G_Q, G_K, G_V, G_R, G_A, D_Q, D_K, D_V, D_IQ, D_IK, D_IW, GATES) = np.cumsum(
    [0, 512, 512, 256, 256, 512, 512, 16, 512, 512, 512, 256, 64, 4]).tolist()
(Q2, K2, V2, F2, CB2, CC2, CI2, GA2, GC2) = np.cumsum([0, 512, 512, 512, 8, 512, 512, 512, 1024]).tolist()

V1 = dict(b_mod=0, c=48, g_norm1=56, g_norm2=64, b_branch_gate=72, gla_b_gate=96, gla_norm_g=98,
          dsa_qnorm_g=99, dsa_knorm_g=100)
V1_ROWS = 101
V2_NAMES = ["g_ffn1_pre_2", "g_ffn1_post_2", "g_mix_pre_2", "g_mix_post_2", "g_ffn2_pre_2", "g_ffn2_post_2"]
CONV_ROW = 48
V2_ROWS = 60


def distance_buckets():
    n = np.maximum(np.arange(640) - 127, 0)
    large = 16 + (np.log(np.maximum(n, 16).astype(np.float32) / 16) / np.float32(np.log(8.0)) * 16).astype(np.int32)
    b = np.where(n < 16, n, np.minimum(large, 31))
    return (np.arange(32)[:, None] == b[None, :]).astype(np.float32)


class PsumWalk:

    def __init__(self, eng, ready, free):
        self.eng, self.ready, self.free = eng, ready, free
        self.g = 0
        self.more = 0

    def claim(self):
        if self.g >= SLOTS:
            self.eng.wait_ge(self.free[self.g % SLOTS], self.g // SLOTS + self.more)
        return self.g % SLOTS

    def made(self, ins):
        ins.then_inc(self.ready[self.g % SLOTS], 1)
        self.g += 1

    def arrive(self):
        self.eng.wait_ge(self.ready[self.g % SLOTS], self.g // SLOTS + 1 + self.more)
        return self.g % SLOTS

    def release(self, ins):
        ins.then_inc(self.free[self.g % SLOTS], 1)
        self.g += 1

    def skip(self, n=1):
        self.g += n

    def wait_released(self, g):
        self.eng.wait_ge(self.free[g % SLOTS], g // SLOTS + 1 + self.more)

    def wait_made(self, g):
        self.eng.wait_ge(self.ready[g % SLOTS], g // SLOTS + 1 + self.more)


class Link:

    def __init__(self, eng, sem):
        self.eng, self.sem, self.n, self.more = eng, sem, 0, 0

    def mark(self, ins):
        self.n += 1
        ins.then_inc(self.sem, 1)
        return self.n

    def wait(self, n=None):
        self.eng.wait_ge(self.sem, (self.n if n is None else n) + self.more)

    def __call__(self, ins):
        self.mark(ins)
        self.wait()


def halves(T):
    return [(0, T)] if T <= 512 else [(0, T // 2), (T // 2, T // 2)]


def build(nc, a, one_hot, out):
    with ExitStack() as ctx:
        BASE = 1280
        names = {}

        def at(name, off, shape, dt=F32):
            names[name] = off
            return nc.alloc_sbuf_tensor_at(name, [P] + list(shape), dt, offset=off)

        def sem(name):
            return ctx.enter_context(nc.semaphore(name))

        PS = ctx.enter_context(nc.psum_tensor("PS", [P, SLOTS, 2, 512], F32))

        B = BASE
        w_raw = at("w_raw", B, [RING, CH]); B += RING * CH * 4
        w_hi = at("w_hi", B, [RING, CH], F32R); B += RING * CH * 4
        w_lo = at("w_lo", B, [RING, CH], F32R); B += RING * CH * 4
        R = at("R", B, [KT, TALL]); B += KT * TALL * 4
        HF_OFF = B
        Hf = at("Hf", B, [KT, TALL]); B += KT * TALL * 4
        HH = at("HH", B, [KT, TALL], F32R); B += KT * TALL * 4
        HL = at("HL", B, [KT, TALL], F32R); B += KT * TALL * 4
        ident = at("ident", B, [P]); B += 512
        ones = at("ones", B, [P]); B += 512
        tri = at("tri", B, [P]); B += 512
        outside = at("outside", B, [P]); B += 512
        C1 = at("C1", B, [P]); B += 512
        C2 = at("C2", B, [P]); B += 512
        modc = at("modc", B, [48]); B += 192
        w_route = at("w_route", B, [KT, 20]); B += 640
        w_forget = at("w_forget", B, [KT, 8]); B += 256
        w_gate2 = at("w_gate2", B, [256]); B += 1024
        rs = at("rs", B, [TALL]); B += TALL * 4
        c_act = at("c_act", B, [KT]); B += 32
        iw = at("iw", B, [NTOK, 4]); B += 64
        b_fox = at("b_fox", B, [8]); B += 32
        relb = at("relb", B, [4]); B += 32
        eps = at("eps", B, [8]); B += 32
        gain1 = at("gain1", B, [KT]); B += 32
        gain2 = at("gain2", B, [KT]); B += 32
        tri2 = at("tri2", B, [CHUNK]); B += 256
        nmax = at("nmax", B, [32]); B += 128
        den = at("den", B, [32]); B += 128
        rden = at("rden", B, [32]); B += 128
        stats = at("stats", B, [NTOK, 6]); B += 96
        mv = at("mv", B, [NTOK, 2]); B += 32
        rstd = at("rstd", B, [NTOK]); B += 32
        ebl = at("ebl", B, [2, 8]); B += 64
        b_route = at("b_route", B, [32]); B += 128
        A0 = B
        room = nc.sbuf_usable_end - A0

        def ar(name, off, shape, dt=F32):
            assert off + int(np.prod(shape)) * 4 <= room, (name, off, room)
            return at(name, A0 + off, shape, dt)

        def hf(name, off, shape, dt=F32):
            assert off + int(np.prod(shape)) * 4 <= KT * TALL * 4
            return at(name, HF_OFF + off, shape, dt)

        u = ar("u", 0, [BT, SEQ])
        w_small = ar("w_small", 0, [KT, 148])
        v = ar("v", 8192, [NTOK, DB])
        gq = ar("gq", 16384, [2, SEQ])
        gk = ar("gk", 20480, [2, SEQ])
        gv = ar("gv", 24576, [NTOK, DB])
        gr = ar("gr", 32768, [BT, SEQ])
        dq = ar("dq", 40960, [BT, SEQ])
        oh_sb = ar("oh_sb", 40960, [640])
        dist_sb = ar("dist_sb", 43520, [640])
        vec_a = ar("vec_a", 46080, [P])
        vec_b = ar("vec_b", 46592, [P])
        meta_sb = ar("meta_sb", 49152, [D])
        dk = ar("dk", 49152, [BT, SEQ])
        dv = ar("dv", 57344, [NTOK, DB])
        relu_s = ar("relu_s", 57344, [2, SEQ])
        iq = ar("iq", 65536, [2, SEQ])
        ik = ar("ik", 69632, [SEQ])
        sc = [None] + [ar(f"sc{i}", 71680 + (0, 1024, 2560)[i - 1], [(i + 1) * P]) for i in (1, 2, 3)]
        keep0 = ar("keep0", 76288, [P])
        ga = rs
        macc = ar("macc", 61440, [2, 256])
        max8 = ar("max8", 76800, [8])
        keep = [keep0] + sc[1:]
        x_tok = hf("x_tok", 0, [NTOK, D])
        mod_raw = hf("mod_raw", 0, [2, KT, 256])
        ws = hf("ws", 0, [4, P])
        wsT = hf("wsT", 2048, [4, P])
        ln_rows = hf("ln_rows", 4096, [2, DB])
        bs_rows = hf("bs_rows", 8192, [4, P])
        mixt = hf("mixt", 10240, [2, SEQ])
        sqh = hf("sqh", 0, [2, SEQ])
        rsh = hf("rsh", 4096, [2, SEQ])
        bias_rev = ar("bias_rev", 8192, [4, SEQ])
        lg1 = hf("lg1", 0, [2, SEQ])
        pr1 = hf("pr1", 4096, [3, SEQ])
        bm = hf("bm", 10240, [SEQ])
        pT1 = hf("pT1", 12288, [2, 4, P])
        Bc = ar("Bc", 65536, [2, SEQ])
        t0 = ar("t0", 69632, [SEQ])
        t1 = ar("t1", 71680, [SEQ])
        t2 = ar("t2", 73728, [SEQ])
        Kp = hf("Kp", 0, [4, SEQ])
        Qp = hf("Qp", 8192, [4, SEQ])
        qe = ar("qe", 8192, [2, SEQ])
        kk = ar("kk", 12288, [2, SEQ])
        kkT = ar("kkT", 49152, [2, NTOK, P])
        attT = ar("attT", 53248, [4, NTOK, CHUNK])
        og = ar("og", 57344, [4, SEQ])
        Sall = ar("Sall", 16384, [8, 2, P])
        YH = ar("YH", 8192, [12, SEQ], F32R)
        YL = ar("YL", 49152, [12, SEQ], F32R)
        sg1 = ar("sg1", 0, [4, SEQ])
        mt1 = ar("mt1", 73728, [2, SEQ])
        yacc = ar("yacc", 0, [KT, TALL])
        ah = ar("ah", 16896, [2, 2, TALL], F32R)
        al = ar("al", 25344, [2, 2, TALL], F32R)
        actf = ar("actf", 33792, [2, TALL])
        sg = ar("sg", 38016, [2, TALL])
        comb = ar("comb", 42240, [N_EXP, SEQ])
        combT = ar("combT", 75008, [SEQ])
        rl = ar("rl", 0, [NTOK, 20])
        rt = ar("rt", 1024, [16, NTOK, 4])
        rc = ar("rc", 2048 + 1024, [NTOK, 16])
        q2 = ar("q2", 0, [4, SEQ])
        k2 = ar("k2", 8192, [4, TALL])
        v2 = ar("v2", 16640, [5, DB])
        pc = ar("pc", 26880, [4, TALL])
        yc2 = ar("yc2", 35328, [4, SEQ])
        negF = ar("negF", 43520, [TALL])
        fz = ar("fz", 45632, [2, TALL])
        ya2 = ar("ya2", 49856, [4, SEQ])
        lg2 = ar("lg2", 58048, [2, TALL])
        pr2 = ar("pr2", 62272, [3, TALL])
        pT2 = ar("pT2", 68608, [2, 5, P])
        YH2 = ar("YH2", 0, [8, SEQ], F32R)
        YL2 = ar("YL2", 16384, [8, SEQ], F32R)
        sg2 = ar("sg2", 58048, [4, SEQ])
        mt2 = ar("mt2", 66240, [2, SEQ])
        o_tok = ar("o_tok", 0, [NTOK, D])

        dist_dram = nc.dram_tensor("dist_dram", (4, 640), F32, kind="Internal").ap()

        ready = [sem(f"psum_ready{s}") for s in range(SLOTS)]
        free = [sem(f"psum_free{s}") for s in range(SLOTS)]
        w_in_sem = [sem(f"chunk_landed{s}") for s in range(RING)]
        hi_done = sem("chunk_hi_done")
        split = sem("chunk_split")
        begun = sem("chunk_begun")
        vec_in = sem("vectors_in")
        x_in = sem("x_in")
        small_in = sem("small_in")
        oh_in = sem("one_hot_in")
        dist_out = sem("dist_out")
        bias_in = sem("bias_in")
        gm_in = sem("gmlp_in")
        mod_in = [sem(f"mod_landed{s}") for s in range(2)]
        mod_used = sem("mod_used")
        consts = sem("consts")
        out_done = sem("out_done")
        cols_ready = sem("columns_ready")
        dist_ready = sem("dist_ready")
        cact_ready = sem("c_act_ready")
        macc_ready = sem("macc_ready")
        sq_ready = sem("squares_ready")
        hraw_ready = sem("h_ready")
        hh_ready = sem("h_hi_ready")
        hl_ready = sem("h_lo_ready")
        act_link = sem("act_link")
        dve_link = sem("dve_link")
        relu_used = sem("relu_used")
        gmv_ready = sem("gmlp_v_ready")
        var_ready = sem("var_ready")
        std_ready = sem("std_ready")
        wsT_ready = sem("wsT_ready")
        hsq_ready = sem("head_squares_ready")
        hn_done = sem("head_norm_done")
        lg_ready = sem("logits_ready")
        p_ready = sem("probs_ready")
        pn_ready = sem("probs_normed")
        gla_dve = sem("gla_factors_ready")
        gla_act = sem("exp_done")
        exp_arg = sem("exp_argument_ready")
        negF_ready = sem("forget_sums_ready")
        inner_done = sem("gla_inner_done")
        y_src = sem("y_ready")
        yh_ready = sem("y_hi_ready")
        yl_ready = sem("y_lo_ready")
        merged_ready = sem("merged_ready")
        moe_act = sem("swiglu_act_ready")
        router_done = sem("router_weights_ready")
        ex_ready = sem("router_exp_argument")
        ex_done = sem("router_exp_done")
        gmlp_done = sem("gmlp_done")
        r_done = sem("residual_done")
        o_ready = sem("out_ready")

        def wk(name):
            return a[name][0].rearrange("(k p) n -> p k n", p=P)

        P1 = [("fm", D_IQ), ("tm", A_V), ("tm", A_V + 256), ("fm", A_U), ("fm", A_U + 256),
              ("tm", G_V), ("tm", G_V + 256), ("fm", G_Q), ("fm", G_K), ("fm", G_R), ("fm", G_R + 256),
              ("fm", D_Q), ("fm", D_Q + 256), ("fm", D_K), ("fm", D_K + 256), ("tm", D_V), ("tm", D_V + 256)]
        MOD1 = 8
        MODN = 24
        MODS_AT = [2] + [1] * 14 + [0] * 2
        SMALL_TILE = 23
        n_p1, n_m1, n_wo, n_moe = len(P1), 18, 4, 3 * N_EXP
        n_ff, n_p2, n_m2 = 3 * FF_UNITS, 12, 12
        P2 = [("fm", CC2), ("fm", CC2 + 256), ("fm", CI2), ("fm", CI2 + 256), ("fm", CB2), ("fm", CB2 + 256),
              ("fm", K2), ("fm", K2 + 256), ("fm", Q2), ("fm", Q2 + 256), ("tm", V2), ("tm", V2 + 256)]
        NCHUNK = n_p1 + n_m1 + n_wo + n_moe + n_ff + n_p2 + n_m2 + n_wo + n_ff

        block = ctx.enter_context(nc.Block())

        @block.sync
        def _(sp):
            count = [0, 0]

            def load(src, shape_k, n, more=0):
                c = count[0]
                if c >= RING:
                    sp.wait_ge(split, c - RING + 1 + more)
                dst = w_raw[:, c % RING, :].rearrange("p (k n) -> p k n", k=shape_k)
                sp.dma_start(dst, src).then_inc(w_in_sem[c % RING], 16)
                count[0] += 1

            def cols(name, c0):
                load(wk(name)[:, :, c0:c0 + 256], KT, 256)

            def load_mod(n):
                if n >= 2:
                    sp.wait_ge(mod_used, n - 1)
                sp.dma_start(mod_raw[:, n % 2, :, :], wk("w_mod")[:, :, 256 * n:256 * n + 256]).then_inc(mod_in[n % 2], 16)

            def row(name, r, n, tile, src=None):
                s = src if src is not None else a[name].rearrange("a (r n) -> (a r) n", n=P)
                sp.dma_start(tile[r:r + n, :], s).then_inc(vec_in, 16)

            sp.dma_start(x_tok[:, :, :], a["x"][0].rearrange("(t p) d -> p t d", p=P)).then_inc(x_in, 16)
            row("b_mod", 0, 48, vec_a)
            row("c", 48, 8, vec_a)
            row("g_norm1", 56, 8, vec_a)
            row("g_norm2", 64, 8, vec_a)
            row("b_branch_gate", 72, 24, vec_a, a["b_branch_gate"].rearrange("a b (r n) -> (a b r) n", n=P))
            row("gla_b_gate", 96, 2, vec_a)
            row("gla_norm_g", 98, 1, vec_a)
            row("dsa_qnorm_g", 99, 1, vec_a)
            row("dsa_knorm_g", 100, 1, vec_a)
            for n, name in enumerate(V2_NAMES):
                row(name, 8 * n, 8, vec_b)
            row("conv_w_2", CONV_ROW, 12, vec_b, a["conv_w_2"].rearrange("a j (r n) -> (a j r) n", n=P))
            sp.dma_start(oh_sb[0:32, :], one_hot).then_inc(oh_in, 16)
            sp.dma_start(relb[0:32, :], a["rel_bias"]).then_inc(oh_in, 16)
            sp.dma_start(meta_sb[0:META, :], a["meta_tokens_2"]).then_inc(oh_in, 16)
            w1 = wk("w_in")
            sp.dma_start(w_small[:, :, 0:16], w1[:, :, G_A:G_A + 16]).then_inc(small_in, 16)
            sp.dma_start(w_small[:, :, 16:80], w1[:, :, D_IK:D_IK + 64]).then_inc(small_in, 16)
            sp.dma_start(w_small[:, :, 80:144], w1[:, :, D_IK:D_IK + 64]).then_inc(small_in, 16)
            sp.dma_start(w_small[:, :, 144:148], w1[:, :, D_IW:D_IW + 4]).then_inc(small_in, 16)
            sp.dma_start(w_gate2[0:16, :], a["gla_w_gate2"][0]).then_inc(small_in, 16)
            sp.dma_start(w_route[:, :, 0:4], wk("w_group")).then_inc(small_in, 16)
            sp.dma_start(w_route[:, :, 4:20], wk("w_router")).then_inc(small_in, 16)
            sp.dma_start(b_route[:, 0:4], a["b_group"][0:1, :].to_broadcast([P, 4])).then_inc(small_in, 16)
            sp.dma_start(b_route[:, 4:20], a["b_router"][0:1, :].to_broadcast([P, 16])).then_inc(small_in, 16)
            sp.dma_start(w_forget[:, :, :], wk("w_in_2")[:, :, F2:F2 + 8]).then_inc(small_in, 16)
            sp.dma_start(b_fox[0:8, 0:1], a["b_forget_2"].rearrange("a h -> h a")).then_inc(small_in, 16)

            for s in range(SLOTS):
                sp.wait_ge(ready[s], 2)
            for n in range(MOD1):
                load_mod(n)
            for c in range(RING):
                cols("w_in", P1[c][1])
            sp.wait_ge(dist_ready, 1)
            sp.dma_start(dist_dram, dist_sb[0:4, :]).then_inc(dist_out, 16)
            sp.wait_ge(ready[SMALL_TILE % SLOTS], SMALL_TILE // SLOTS + 1)
            m = MOD1
            for n, k in enumerate(MODS_AT):
                for _ in range(k):
                    load_mod(m)
                    m += 1
                if RING + n < n_p1:
                    cols("w_in", P1[RING + n][1])
            sp.wait_ge(mod_used, MODN)
            sp.dma_start(ws[:, :, :], a["gmlp_w_s"][0].rearrange("g t s -> t g s")).then_inc(gm_in, 16)
            sp.dma_start(ln_rows[:, 0, :], a["gmlp_ln_g"][0:1, :].to_broadcast([P, DB])).then_inc(gm_in, 16)
            sp.dma_start(ln_rows[:, 1, :], a["gmlp_ln_b"][0:1, :].to_broadcast([P, DB])).then_inc(gm_in, 16)
            sp.dma_start(bs_rows[:, :, :], a["gmlp_b_s"].rearrange("a g t -> a (g t)").to_broadcast([P, 4 * P])
                         .rearrange("p (g t) -> p g t", g=4)).then_inc(gm_in, 16)

            def merge_loads(w_gate, gate0, w_up, n_br):
                for mq in range(2):
                    c0 = count[0]
                    with sp.Fori(0, n_br) as n:
                        count[0] = c0
                        for j in range(2):
                            base = gate0 + 512 * mq + 256 * j
                            load(wk(w_gate)[:, :, bass.ds(n * D + base, 256)], KT, 256, n * 3)
                        load(w_up(n, mq), BT, 512, n * 3)
                    count[0] = c0 + 3 * n_br

            merge_loads("w_in", GATES, lambda n, mq: a["w_branch"][0].rearrange("b (k p) n -> p b k n", p=P)[
                :, bass.ds(n, 1), :, 512 * mq:512 * mq + 512].rearrange("p b k n -> p (b k) n"), 3)
            for j in range(4):
                cols("w_out", 256 * j)

            def swiglu_loads(gate, up, down, units):
                load(gate(0), KT, 256)
                load(up(0), KT, 256)
                c0 = count[0]
                with sp.Fori(0, units - 1) as i:
                    count[0] = c0
                    load(gate(i + 1), KT, 256, i * 3)
                    load(up(i + 1), KT, 256, i * 3)
                    load(down(i), 2, D, i * 3)
                count[0] = c0 + 3 * (units - 1)
                load(down(units - 1), 2, D)

            swiglu_loads(lambda e: a["w_exp_gate"][0].rearrange("e (k p) f -> p e k f", p=P)[:, bass.ds(e, 1)].rearrange("p e k f -> p (e k) f"),
                         lambda e: a["w_exp_up"][0].rearrange("e (k p) f -> p e k f", p=P)[:, bass.ds(e, 1)].rearrange("p e k f -> p (e k) f"),
                         lambda e: a["w_exp_down"][0].rearrange("e (k p) f -> p e k f", p=P)[:, bass.ds(e, 1)].rearrange("p e k f -> p (e k) f"),
                         N_EXP)

            def ffn_loads(w_i, w_o):
                swiglu_loads(lambda e: wk(w_i)[:, :, bass.ds(e * 256, 256)],
                             lambda e: wk(w_i)[:, :, bass.ds(e * 256 + D_FF, 256)],
                             lambda e: wk(w_o)[:, bass.ds(e * 2, 2), :], FF_UNITS)

            ffn_loads("w_ffn1_in_2", "w_ffn1_out_2")
            for _, c0 in P2:
                cols("w_in_2", c0)
            for mq in range(2):
                for n in range(2):
                    for j in range(2):
                        cols("w_in_2", GA2 + D * n + 512 * mq + 256 * j)
                    load(wk(("w_attn_branch_2", "w_conv_branch_2")[n])[:, :, 512 * mq:512 * mq + 512], BT, 512)
            for j in range(4):
                cols("w_out_2", 256 * j)
            ffn_loads("w_ffn2_in_2", "w_ffn2_out_2")
            assert count[0] == NCHUNK
            for t in range(NTOK):
                sp.wait_ge(o_ready, 2 * (t + 1))
                sp.dma_start(out[0, P * t:P * t + P, :], o_tok[:, t, :]).then_inc(out_done, 16)
            sp.wait_ge(out_done, 16 * NTOK)

        @block.gpsimd
        def _(pool):
            pool.memset(ident[:, :], 0.0).then_inc(consts, 1)
            pool.memset(ones[:, :], 1.0).then_inc(consts, 1)
            pool.memset(outside[:, :], 0.0).then_inc(consts, 1)
            pool.memset(eps[:, 0:1], EPS).then_inc(consts, 1)
            pool.memset(eps[:, 1:2], 1.0).then_inc(consts, 1)
            pool.wait_ge(consts, 5)
            pool.affine_select(out=ident[:, :], in_=ident[:, :], compare_op=ALU.not_equal, fill=1.0, base=0,
                               pattern=[[-1, P]], channel_multiplier=1).then_inc(consts, 1)
            pool.affine_select(out=tri[:, :], in_=ones[:, :], compare_op=ALU.is_ge, fill=0.0, base=0,
                               pattern=[[1, P]], channel_multiplier=-1).then_inc(consts, 1)
            pool.affine_select(out=outside[:, :], in_=outside[:, :], compare_op=ALU.is_ge, fill=OUTSIDE, base=0,
                               pattern=[[-1, P]], channel_multiplier=1).then_inc(consts, 1)

            def split_chunk(c, s, more=0):
                pool.wait_ge(hi_done, c + 1 + more * RING)
                pool.tensor_tensor(w_lo[:, s, :], w_raw[:, s, :], w_hi[:, s, :].bitcast(F32), ALU.subtract).then_inc(split, 1)

            for c in range(RING):
                split_chunk(c, c)
            rounds = (NCHUNK - RING) // RING
            with pool.Fori(0, rounds) as i:
                for s in range(RING):
                    split_chunk(RING + s, s, i)
            for c in range(RING * (rounds + 1), NCHUNK):
                split_chunk(c, c % RING)

        @block.tensor
        def _(pe):
            W = PsumWalk(pe, ready, free)
            mm = nc.tensor.matmul
            cur = {"c": 0, "more": 0}

            def begin_chunk():
                c = cur["c"]
                pe.wait_ge(split, c + 1 + cur["more"])
                cur["c"] += 1
                cur["fresh"] = True
                return c % RING

            def product(o, l, r, **k):
                ins = mm(o, l, r, **k)
                if cur["fresh"]:
                    ins.then_inc(begun, 1)
                    cur["fresh"] = False
                return ins

            def three(outs, lhs, rhs, first, last):
                for n, (l, r) in enumerate(((0, 0), (0, 1), (1, 0))):
                    for o, cs in outs:
                        ins = product(o, lhs[l], rhs[r][:, cs], start=first and n == 0, stop=last and n == 2)
                return ins

            def outs_of(s, T):
                return [(PS[:, s, b, 0:n], slice(c0, c0 + n)) for b, (c0, n) in enumerate(halves(T))]

            def fm_chunk(nk, mt, rh, rl_, T):
                s_w = begin_chunk()
                hi = w_hi[:, s_w, :].rearrange("p (k n) -> p k n", k=nk)
                lo = w_lo[:, s_w, :].rearrange("p (k n) -> p k n", k=nk)
                for m in range(mt):
                    s = W.claim()
                    for k in range(nk):
                        cs = slice(P * m, P * m + P)
                        ins = three(outs_of(s, T), (hi[:, k, cs], lo[:, k, cs]), (rh(k), rl_(k)), k == 0, k == nk - 1)
                    W.made(ins)

            def h_operands(t0_, T):
                return (lambda k: HH[:, k, t0_:t0_ + T]), (lambda k: HL[:, k, t0_:t0_ + T])

            def tm_chunk(tiles):
                s_w = begin_chunk()
                hi = w_hi[:, s_w, :].rearrange("p (k n) -> p k n", k=KT)
                lo = w_lo[:, s_w, :].rearrange("p (k n) -> p k n", k=KT)
                for t_0, tn in tiles:
                    s = W.claim()
                    for k in range(KT):
                        for n, (l, r) in enumerate(((HH, hi), (HH, lo), (HL, hi))):
                            ins = product(PS[0:tn, s, 0, 0:256], l[:, k, t_0:t_0 + tn], r[:, k, :],
                                          start=k == 0 and n == 0, stop=k == KT - 1 and n == 2)
                    W.made(ins)

            hcount = {"sq": 0, "hl": 0, "hsq": 0, "mod": 0}

            def norm(T):
                s = W.claim()
                for k in range(KT):
                    hcount["sq"] += 1
                    pe.wait_ge(sq_ready, hcount["sq"])
                    for b, (c0, n) in enumerate(halves(T)):
                        ins = mm(PS[:, s, b, 0:n], ones[:, :], Hf[:, k, c0:c0 + n], start=k == 0, stop=k == KT - 1)
                W.made(ins)

            def await_h():
                hcount["hl"] += KT
                pe.wait_ge(hl_ready, hcount["hl"])

            def mod_tile():
                hcount["mod"] += 1
                n = hcount["mod"] - 1
                pe.wait_ge(macc_ready, n + 1)
                s = W.claim()
                for m in range(2):
                    ins = mm(PS[:, s, 0, m:m + 1], macc[:, n % 2, P * m:P * m + P], ones[:, 0:1], start=True, stop=True)
                W.made(ins)

            pe.wait_ge(consts, 8)
            pe.wait_ge(x_in, 16)
            for k in range(KT):
                s = W.claim()
                for t in range(NTOK):
                    ins = nc.tensor.transpose(PS[:, s, 0, P * t:P * t + P], x_tok[:, t, P * k:P * k + P], ident[:, :])
                W.made(ins)
            pe.wait_ge(vec_in, 16 * 16)
            for rows, src in ((V1_ROWS, vec_a), (V2_ROWS, vec_b)):
                s = W.claim()
                W.made(nc.tensor.transpose(PS[:, s, 0, 0:rows], src[0:rows, :], ident[0:rows, 0:rows]))
            pe.wait_ge(oh_in, 48)
            s = W.claim()
            for k in range(KT):
                ins = nc.tensor.transpose(PS[:, s, 0, META * k:META * k + META], meta_sb[0:META, P * k:P * k + P],
                                          ident[0:META, 0:META])
            W.made(ins)
            s = W.claim()
            mm(PS[0:4, s, 0, 0:512], relb[0:32, :], oh_sb[0:32, 0:512], start=True, stop=True)
            W.made(mm(PS[0:4, s, 1, 0:128], relb[0:32, :], oh_sb[0:32, 512:640], start=True, stop=True))
            for n in range(MOD1):
                mod_tile()
            norm(SEQ)
            await_h()
            pe.wait_ge(small_in, 16 * 11)
            for c0, n in ((0, 16), (16, 128)):
                s = W.claim()
                for k in range(KT):
                    ins = mm(PS[0:n, s, 0, :], w_small[:, k, c0:c0 + n], Hf[:, k, 0:SEQ], start=k == 0, stop=k == KT - 1)
                W.made(ins)
            s = W.claim()
            for t in range(NTOK):
                for k in range(KT):
                    ins = mm(PS[:, s, 0, 4 * t:4 * t + 4], Hf[:, k, P * t:P * t + P], w_small[:, k, 144:148],
                             start=k == 0, stop=k == KT - 1)
            W.made(ins)
            rh, rlo = h_operands(0, SEQ)
            tok_tiles = [(P * t, P) for t in range(NTOK)]
            for n, (kind, _) in enumerate(P1):
                if kind == "fm":
                    fm_chunk(KT, 2, rh, rlo, SEQ)
                else:
                    tm_chunk(tok_tiles)
                if n == 0:
                    W.wait_released(W.g - 1)
                    W.wait_released(W.g - 2)
                    for i in range(1, NTOK):
                        for h in range(4):
                            s = W.claim()
                            b = 64 * (h % 2)
                            W.made(mm(PS[:, s, 0, 0:(i + 1) * P], iq[b:b + 64, h // 2, P * i:P * i + P],
                                      ik[b:b + 64, 0:(i + 1) * P], start=True, stop=True))
                for _ in range(MODS_AT[n]):
                    mod_tile()

            pe.wait_ge(gm_in, 64)
            s = W.claim()
            for g in range(4):
                ins = nc.tensor.transpose(PS[:, s, 0, P * g:P * g + P], ws[:, g, :], ident[:, :])
            W.made(ins)
            pe.wait_ge(wsT_ready, 1)
            pe.wait_ge(gmv_ready, 1)
            for g in range(4):
                s = W.claim()
                for t in range(NTOK):
                    ins = mm(PS[:, s, 0, P * t:P * t + P], v[:, t, P * g:P * g + P], wsT[:, g, :], start=True, stop=True)
                W.made(ins)

            def head_norms(n):
                for _ in range(n):
                    s = W.claim()
                    hcount["hsq"] += 1
                    pe.wait_ge(hsq_ready, hcount["hsq"])
                    W.made(mm(PS[:, s, 0, :], ones[:, :], sqh[:, (hcount["hsq"] - 1) % 2, :], start=True, stop=True))

            att = {"n": 0}

            def attention(combos, logits, keys, pr, pT, values, o):
                N = len(combos)
                for n in range(N + 3):
                    if n < N:
                        s = W.claim()
                        W.made(logits(s, *combos[n]))
                    if 0 <= n - 2 < N:
                        i, h = combos[n - 2]
                        att["n"] += 1
                        pe.wait_ge(pn_ready, att["n"])
                        s = W.claim()
                        for c0, kt, kn in keys(i):
                            bank, col = (0, P * kt) if kt < 4 else (1, 0)
                            ins = nc.tensor.transpose(PS[0:kn, s, bank, col:col + P], pr[:, (n - 2) % 3, c0:c0 + kn], ident[:, :])
                        att[n - 2] = W.g
                        W.made(ins)
                    if 0 <= n - 3 < N:
                        i, h = combos[n - 3]
                        W.wait_released(att[n - 3])
                        s = W.claim()
                        ks = keys(i)
                        for x, (c0, kt, kn) in enumerate(ks):
                            ins = mm(o(s, h), values(kt, kn, h), pT[0:kn, (n - 3) % 2, kt, :], start=x == 0, stop=x == len(ks) - 1)
                        W.made(ins)

            head_norms(8)
            pe.wait_ge(hn_done, 8)
            combos1 = [(i, h) for i in range(NTOK) for h in range(4)]
            attention(combos1,
                      lambda s, i, h: mm(PS[:, s, 0, 0:(i + 1) * P], dq[:, h, P * i:P * i + P], dk[:, h, 0:(i + 1) * P],
                                         start=True, stop=True),
                      lambda i: [(P * j, j, P) for j in range(i + 1)], pr1, pT1,
                      lambda kt, kn, h: dv[:, kt, P * h:P * h + P], lambda s, h: PS[:, s, 0, 0:P])

            for j in range(2):
                s = W.claim()
                W.made(mm(PS[:, s, 0, :], w_gate2[0:16, P * j:P * j + P], ga[0:16, 0:SEQ], start=True, stop=True))
            for j in range(2):
                pe.wait_ge(gla_dve, j + 1)
                for hh in range(2):
                    s = W.claim()
                    hp = slice(64 * hh, 64 * hh + 64)
                    for c in range(8):
                        op = slice(64 * (c % 2), 64 * (c % 2) + 64)
                        for q in range(4):
                            ins = mm(PS[op, s, 0, CHUNK * (c // 2):CHUNK * (c // 2) + CHUNK], Kp[hp, q, CHUNK * c:CHUNK * c + CHUNK],
                                     Qp[hp, q, CHUNK * c:CHUNK * c + CHUNK], start=q == 0, stop=q == 3)
                    W.made(ins)
                s = W.claim()
                for t in range(NTOK):
                    ins = nc.tensor.transpose(PS[:, s, 0, P * t:P * t + P], kk[:, j, P * t:P * t + P], ident[:, :])
                W.made(ins)
            W.wait_released(W.g - 1)
            W.wait_released(W.g - 4)
            for c in range(7):
                s = W.claim()
                cp = slice(64 * (c % 2), 64 * (c % 2) + 64)
                for j in range(2):
                    for hh in range(2):
                        h = 2 * j + hh
                        ins = mm(PS[64 * hh:64 * hh + 64, s, 0, P * j:P * j + P], kkT[cp, j, c // 2, 64 * hh:64 * hh + 64],
                                 gv[cp, c // 2, P * h:P * h + P], start=True, stop=True)
                W.made(ins)
            pe.wait_ge(gla_dve, 3)
            for h in range(4):
                s = W.claim()
                j, hp = h // 2, slice(64 * (h % 2), 64 * (h % 2) + 64)
                for c in (0, 2, 4, 6, 1, 3, 5, 7):
                    cp = slice(64 * (c % 2), 64 * (c % 2) + 64)
                    ins = mm(PS[:, s, c % 2, CHUNK * (c // 2):CHUNK * (c // 2) + CHUNK], gv[cp, c // 2, P * h:P * h + P],
                             attT[cp, h, c // 2, :], start=c < 2, stop=False, skip_group_check=True)
                ins.then_inc(inner_done, 1)
                pe.wait_ge(inner_done, h + 1)
                for c in range(1, 8):
                    ins = mm(PS[:, s, c % 2, CHUNK * (c // 2):CHUNK * (c // 2) + CHUNK], Sall[hp, c, j, :],
                             qe[hp, j, CHUNK * c:CHUNK * c + CHUNK], start=False, stop=True, skip_group_check=True)
                W.made(ins)
            head_norms(4)

            ycount = {"yl": 0}

            def merge(n_br, yh, yl, t0_):
                rh_, rl_ = h_operands(t0_, SEQ)
                for mq in range(2):
                    c0, g0 = cur["c"], W.g

                    def body(n, n_static):
                        for _ in range(2):
                            fm_chunk(KT, 2, rh_, rl_, SEQ)
                        if n_static is not None:
                            if mq == 0 and n_static == 0:
                                ycount["yl"] += BT * n_br
                                pe.wait_ge(yl_ready, ycount["yl"])
                        fm_chunk(BT, 4, lambda k: yk(yh, n, k), lambda k: yk(yl, n, k), SEQ)

                    def yk(y, n, k):
                        if isinstance(n, int):
                            return y[:, BT * n + k, :]
                        return y[:, bass.ds(n * BT + k, 1), :].rearrange("p a n -> p (a n)")

                    body(0, 0)
                    with pe.Fori(0, n_br - 1) as i:
                        cur["c"], W.g = c0 + 3, g0 + 8
                        cur["more"], W.more = i * 3, i * 2
                        body(i + 1, None)
                    cur["c"], W.g = c0 + 3 * n_br, g0 + 8 * n_br
                    cur["more"], W.more = 0, 0

            merge(3, YH, YL, 0)

            def out_projection():
                await_h()
                rh_, rl_ = h_operands(0, SEQ)
                for _ in range(4):
                    fm_chunk(KT, 2, rh_, rl_, SEQ)

            out_projection()

            norm(SEQ)
            await_h()
            s = W.claim()
            for t in range(NTOK):
                for k in range(KT):
                    ins = mm(PS[:, s, 0, 20 * t:20 * t + 20], Hf[:, k, P * t:P * t + P], w_route[:, k, :],
                             start=k == 0, stop=k == KT - 1)
            W.made(ins)
            pe.wait_ge(router_done, 1)
            s = W.claim()
            for t in range(NTOK):
                ins = nc.tensor.transpose(PS[0:16, s, 0, P * t:P * t + P], rc[:, t, :], ident[:, :])
            W.made(ins)
            W.wait_released(W.g - 1)
            for e in range(N_EXP):
                s = W.claim()
                W.made(mm(PS[:, s, 0, :], ident[0:16, e:e + 1].to_broadcast([16, P]), combT[0:16, :], start=True, stop=True))

            units_done = {"n": 0}

            def swiglu(units, T, t0_):
                rh_, rl_ = h_operands(t0_, T)
                base = units_done["n"]

                def up():
                    fm_chunk(KT, 2, rh_, rl_, T)
                    fm_chunk(KT, 2, rh_, rl_, T)

                def down(n, par, more=0):
                    pe.wait_ge(moe_act, base + n + 1 + more)
                    fm_chunk(2, KT, lambda k: ah[:, par, k, 0:T], lambda k: al[:, par, k, 0:T], T)

                up()
                c0, g0 = cur["c"], W.g
                pairs = (units - 1) // 2
                with pe.Fori(0, pairs) as i:
                    cur["c"], W.g = c0, g0
                    cur["more"], W.more = i * 6, i * 6
                    for par in range(2):
                        up()
                        down(par, par, i * 2)
                cur["c"], W.g = c0 + 6 * pairs, g0 + 24 * pairs
                cur["more"], W.more = 0, 0
                for n in range(2 * pairs, units):
                    if n + 1 < units:
                        up()
                    down(n, n % 2)
                units_done["n"] += units

            swiglu(N_EXP, SEQ, 0)

            norm(TALL)
            await_h()
            swiglu(FF_UNITS, TALL, 0)
            norm(TALL)
            norm(TALL)
            await_h()
            s = W.claim()
            for k in range(KT):
                for b, (c0, n) in enumerate(halves(TALL)):
                    ins = mm(PS[0:8, s, b, 0:n], w_forget[:, k, :], Hf[:, k, c0:c0 + n], start=k == 0, stop=k == KT - 1)
            W.made(ins)
            pe.wait_ge(negF_ready, 1)
            for h in range(8):
                s = W.claim()
                for b, (c0, n) in enumerate(halves(TALL)):
                    ins = mm(PS[:, s, b, 0:n], ident[0:8, h:h + 1].to_broadcast([8, P]), negF[0:8, c0:c0 + n], start=True, stop=True)
                W.made(ins)
            tok5 = [(META + P * t, P) for t in range(NTOK)] + [(0, META)]
            full, real = h_operands(0, TALL), h_operands(META, SEQ)
            for kind, c0 in P2:
                if kind == "tm":
                    tm_chunk(tok5)
                elif c0 in (CB2, CB2 + 256, Q2, Q2 + 256):
                    fm_chunk(KT, 2, *real, SEQ)
                else:
                    fm_chunk(KT, 2, *full, TALL)

            def fox_logits(s, i, h):
                b = 64 * (h % 2)
                n_all = META + P * (i + 1)
                for bank, c0, n in ((0, 0, min(512, n_all)), (1, 512, n_all - 512)):
                    if n > 0:
                        ins = mm(PS[:, s, bank, 0:n], q2[b:b + 64, h // 2, P * i:P * i + P], k2[b:b + 64, h // 2, c0:c0 + n],
                                 start=True, stop=True)
                return ins

            combos2 = [(i, h) for i in range(NTOK) for h in range(8)]
            W.wait_released(W.g - 1)
            W.wait_released(W.g - 2)
            W.wait_released(W.g - 3)
            W.wait_released(W.g - 4)
            attention(combos2, fox_logits, lambda i: [(0, 4, META)] + [(META + P * j, j, P) for j in range(i + 1)],
                      pr2, pT2, lambda kt, kn, h: v2[0:kn, kt, 64 * h:64 * h + 64],
                      lambda s, h: PS[64 * (h % 2):64 * (h % 2) + 64, s, 0, 0:P])
            merge(2, YH2, YL2, META)
            out_projection()
            norm(SEQ)
            norm(SEQ)
            await_h()
            swiglu(FF_UNITS, SEQ, 0)
            norm(SEQ)
            pe.wait_ge(r_done, 1)
            for t in range(NTOK):
                for half in range(2):
                    s = W.claim()
                    for k in range(4):
                        ins = nc.tensor.transpose(PS[:, s, 0, P * k:P * k + P],
                                                  R[:, 4 * half + k, META + P * t:META + P * t + P], ident[:, :])
                    W.made(ins)
            assert cur["c"] == NCHUNK

        @block.scalar
        def _(act):
            W = PsumWalk(act, ready, free)
            L = Link(act, act_link)
            af = nc.scalar.activation
            n_ = {"hraw": 0, "hh": 0, "hn": 0, "lg": 0, "ysrc": 0, "merged": 0, "std": 0}

            def ps(s, T=SEQ):
                return PS[:, s, 0, 0:T] if T <= 512 else PS[:, s, 0:2, 0:T // 2]

            def sv(ap, T):
                return ap if T <= 512 else ap.rearrange("p (b n) -> p b n", b=2)

            def evac(out_, func=ACT.Copy, src=None, **k):
                s = W.arrive()
                W.release(af(out_, ps(s) if src is None else src(s), func, **k))

            def norm(T, shift=None, split=True):
                s = W.arrive()
                W.release(af(sv(rs[:, 0:T], T), ps(s, T), ACT.Sqrt, scale=1.0 / D, bias=eps[:, 0:1]))
                if not split:
                    return
                for k in range(KT):
                    n_["hraw"] += 1
                    act.wait_ge(hraw_ready, n_["hraw"])
                    if shift is not None:
                        L(af(Hf[:, k, 0:T], Hf[:, k, 0:T], ACT.Identity, bias=shift(k)))
                    af(HH[:, k, 0:T], Hf[:, k, 0:T], ACT.Copy).then_inc(hh_ready, 1)

            hi = {"c": 0, "rounds": 0}

            def next_hi():
                c = hi["c"]
                if c >= NCHUNK:
                    return
                rounds = hi["rounds"]
                act.wait_ge(w_in_sem[c % RING], 16 * (c // RING + 1) + rounds * 16)
                if c >= RING:
                    act.wait_ge(begun, c - 1 + rounds * RING)
                af(w_hi[:, c % RING, :], w_raw[:, c % RING, :], ACT.Copy).then_inc(hi_done, 1)
                hi["c"] += 1

            for k in range(KT):
                s = W.arrive()
                ins = af(R[:, k, META:TALL], ps(s), ACT.Copy)
                W.release(ins)
            W.skip(2)
            s = W.arrive()
            W.release(af(R[:, :, 0:META], PS[:, s, 0, 0:KT * META].rearrange("p (k t) -> p k t", t=META), ACT.Copy))
            W.skip(1)
            act.wait_ge(cols_ready, 1)
            af(c_act[:, :], C1[:, V1["c"]:V1["c"] + KT], ACT.Silu).then_inc(cact_ready, 1)
            W.skip(MOD1)
            norm(SEQ, lambda k: modc[:, k:k + 1])
            next_hi()
            next_hi()
            evac(ga[0:16, 0:SEQ], src=lambda s: PS[0:16, s, 0, :])
            evac(ik[:, :])
            evac(iw[:, :, :], src=lambda s: PS[:, s, 0, 0:16].rearrange("p (t h) -> p t h", h=4))

            def tm(dst, c0, func=ACT.Copy):
                for t in range(NTOK):
                    evac(dst[:, t, c0:c0 + 256], func, src=lambda s: PS[:, s, 0, 0:256])

            def fm(dst, m0, func=ACT.Copy):
                for m in range(2):
                    evac(dst[:, m0 + m, :], func)

            plan = {D_IQ: lambda: fm(iq, 0), A_V: lambda: tm(v, 0, ACT.Gelu_apprx_tanh),
                    A_V + 256: lambda: tm(v, 256, ACT.Gelu_apprx_tanh), A_U: lambda: fm(u, 0, ACT.Gelu_apprx_tanh),
                    A_U + 256: lambda: fm(u, 2, ACT.Gelu_apprx_tanh), G_V: lambda: tm(gv, 0), G_V + 256: lambda: tm(gv, 256),
                    G_Q: lambda: fm(gq, 0), G_K: lambda: fm(gk, 0), G_R: lambda: fm(gr, 0, ACT.Silu),
                    G_R + 256: lambda: fm(gr, 2, ACT.Silu), D_Q: lambda: fm(dq, 0), D_Q + 256: lambda: fm(dq, 2),
                    D_K: lambda: fm(dk, 0), D_K + 256: lambda: fm(dk, 2), D_V: lambda: tm(dv, 0), D_V + 256: lambda: tm(dv, 256)}
            for n, (_, c0) in enumerate(P1):
                next_hi()
                if n == 15:
                    act.wait_ge(relu_used, 12)
                plan[c0]()
                if n == 0:
                    for x in range(12):
                        if x >= 2:
                            act.wait_ge(relu_used, x - 1)
                        s = W.arrive()
                        w = (x // 4 + 2) * P
                        W.release(af(relu_s[:, x % 2, 0:w], PS[:, s, 0, 0:w], ACT.Relu))
                W.skip(MODS_AT[n])

            evac(wsT[:, :, :], src=lambda s: PS[:, s, 0, :].rearrange("p (g t) -> p g t", g=4))
            act.wait_ge(var_ready, 1)
            af(rstd[:, :], mv[:, :, 1], ACT.Sqrt, bias=eps[:, 0:1]).then_inc(std_ready, 1)
            W.skip(4)

            def head_norms(count):
                for _ in range(count):
                    n = n_["hn"]
                    if n >= 2:
                        act.wait_ge(hn_done, n - 1)
                    s = W.arrive()
                    W.release(af(rsh[:, n % 2, :], ps(s), ACT.Sqrt, scale=1.0 / P, bias=eps[:, 0:1]))
                    n_["hn"] += 1

            def attention(combos, width, lg, pr, scale, pT, keys, dst, o):
                N = len(combos)
                for n in range(N + 3):
                    if n < N:
                        i, h = combos[n]
                        W.skip(1)
                        n_["lg"] += 1
                        act.wait_ge(lg_ready, n_["lg"])
                        w, c = width(i), n % 32
                        af(pr[:, n % 3, 0:w], lg[:, n % 2, 0:w], ACT.Exp, bias=nmax[:, c:c + 1], scale=scale,
                           accum_out=den[:, c:c + 1]).then_inc(p_ready, 1)
                    if 0 <= n - 2 < N:
                        i, h = combos[n - 2]
                        s = W.arrive()
                        par = (n - 2) % 2
                        if keys:
                            L.mark(af(pT[0:META, par, 4, :], PS[0:META, s, 1, 0:P], ACT.Copy))
                        W.release(af(pT[:, par, 0:i + 1, :], PS[:, s, 0, 0:(i + 1) * P].rearrange("p (k t) -> p k t", t=P), ACT.Copy))
                    if 0 <= n - 3 < N:
                        i, h = combos[n - 3]
                        s = W.arrive()
                        W.release(af(dst(i, h), o(s, h), ACT.Copy))

            act.wait_ge(dist_out, 16)
            act.wait_ge(gmlp_done, 1)
            for h in range(4):
                act.dma_start(bias_rev[:, h, :], bass.AP(dist_dram.tensor, 640 * h, [[1, P], [1, SEQ]])).then_inc(bias_in, 16)
            head_norms(8)
            combos1 = [(i, h) for i in range(NTOK) for h in range(4)]
            attention(combos1, lambda i: (i + 1) * P, lg1, pr1, 1.0, pT1, False,
                      lambda i, h: dq[:, h, P * i:P * i + P], lambda s, h: PS[:, s, 0, 0:P])

            for j in range(2):
                s = W.arrive()
                W.release(af(Bc[:, j, :], ps(s), ACT.Identity, bias=C1[:, V1["gla_b_gate"] + j:V1["gla_b_gate"] + j + 1]))
                W.wait_released(W.g - 1)
                tt = (t0, t1)[j]
                L(af(tt[:, :], Bc[:, j, :], ACT.Abs))
                L(af(tt[:, :], tt[:, :], ACT.Exp, scale=-1.0))
                af(tt[:, :], tt[:, :], ACT.Ln, bias=eps[:, 1:2]).then_inc(gla_act, 1)
            seq = 0
            for j in range(2):
                for _ in range(7):
                    seq += 1
                    act.wait_ge(exp_arg, seq)
                    b = (t0, t1, t2)[(seq - 1) % 3]
                    if (seq - 1) % 7 >= 3:
                        q = (seq - 1) % 7 - 3
                        bb = b[:, :].rearrange("p (c t) -> p c t", c=8)[:, :, SUB * q:CHUNK]
                    else:
                        bb = b[:, :]
                    af(bb, bb, ACT.Exp, scale=1.0 / 16).then_inc(gla_act, 1)
                W.skip(2)
                s = W.arrive()
                W.release(af(kkT[:, j, :, :], PS[:, s, 0, :].rearrange("p (t d) -> p t d", t=NTOK), ACT.Copy))
            act.wait_ge(exp_arg, seq + 1)
            af(ebl[:, :, :], ebl[:, :, :], ACT.Exp, scale=1.0 / 16).then_inc(gla_act, 1)
            W.skip(7)
            for h in range(4):
                evac(og[:, h, :].rearrange("p (c b t) -> p b c t", b=2, t=CHUNK),
                     src=lambda s: PS[:, s, :, 0:SEQ // 2].rearrange("p b (c t) -> p b c t", t=CHUNK))
            head_norms(4)

            def merge(srcs, yh, sg_, n_br, bias):
                n_["ysrc"] += 1
                act.wait_ge(y_src, n_["ysrc"])
                for n, y in enumerate(srcs):
                    af(yh[:, n, :], y, ACT.Copy).then_inc(yh_ready, 1)
                for mq in range(2):
                    g0 = W.g

                    def body(n):
                        for m in range(4):
                            if m % 2 == 0:
                                next_hi()
                            if not (mq == 0 and isinstance(n, int)):
                                W.wait_released(g_base[0] - 4 + m)
                            k = {} if bias is None else {"bias": bias(n, 4 * mq + m)}
                            evac(sg_[:, m, :], ACT.Sigmoid, **k)
                        next_hi()
                        W.skip(4)

                    g_base = [g0]
                    c0 = hi["c"]
                    if mq == 0:
                        act.wait_ge(yl_ready, n_["yl"])
                    body(0)
                    with act.Fori(0, n_br - 1) as i:
                        W.g = g0 + 8
                        g_base[0] = g0 + 8
                        W.more = i * 2
                        hi["c"], hi["rounds"] = c0 + 3, i
                        body(i + 1)
                    W.more = 0
                    hi["c"], hi["rounds"] = c0 + 3 * n_br, 0
                    W.g = g0 + 8 * n_br

            def merged_split():
                n_["merged"] += 1
                act.wait_ge(merged_ready, n_["merged"])
                for k in range(KT):
                    af(HH[:, k, 0:SEQ], Hf[:, k, 0:SEQ], ACT.Copy).then_inc(hh_ready, 1)

            n_["yl"] = 12
            bcol = V1["b_branch_gate"]

            def gate_bias(n, m):
                if isinstance(n, int):
                    return C1[:, bcol + KT * n + m:bcol + KT * n + m + 1]
                return C1[:, bass.ds(n * KT + bcol + m, 1)]

            merge([u[:, k, :] for k in range(4)] + [gr[:, k, :] for k in range(4)] + [dq[:, k, :] for k in range(4)],
                  YH, sg1, 3, gate_bias)
            merged_split()
            for _ in range(4):
                next_hi()
            W.skip(8)

            norm(SEQ, lambda k: modc[:, 24 + k:25 + k])
            W.skip(1)
            act.wait_ge(ex_ready, 1)
            L.mark(af(rt[:, 0, :, :], rt[:, 0, :, :], ACT.Exp))
            af(rt[:, 15, :, 0:1], rt[:, 15, :, 0:1], ACT.Exp).then_inc(ex_done, 1)
            evac(combT[0:16, :], src=lambda s: PS[0:16, s, 0, :])
            for e in range(N_EXP):
                evac(comb[:, e, :])

            def swiglu(units, T, last=False):
                def gates(waits):
                    b = W.g
                    next_hi()
                    for m in range(2):
                        if waits:
                            W.wait_released(b - 10 + m)
                        s = W.arrive()
                        W.release(af(sv(sg[:, m, 0:T], T), ps(s, T), ACT.Silu))
                    next_hi()
                    W.skip(2)

                gates(False)
                g0, c0 = W.g, hi["c"]
                W.wait_released(g0 - 2)
                W.wait_released(g0 - 1)
                pairs = (units - 1) // 2 - last
                with act.Fori(0, pairs) as i:
                    W.g, W.more = g0, i * 6
                    hi["c"], hi["rounds"] = c0, i * 2
                    for _ in range(2):
                        gates(True)
                        next_hi()
                        W.skip(KT)
                W.g, W.more = g0 + 24 * pairs, 0
                hi["c"], hi["rounds"] = c0 + 6 * pairs, 0
                for n in range(2 * pairs, units):
                    if n + 1 < units:
                        gates(True)
                    next_hi()
                    W.skip(KT)

            swiglu(N_EXP, SEQ)
            norm(TALL)
            swiglu(FF_UNITS, TALL)
            norm(TALL, split=False)
            norm(TALL)
            s = W.arrive()
            W.release(af(fz[0:8, 0, :].rearrange("p (b n) -> p b n", b=2), PS[0:8, s, 0:2, 0:TALL // 2], ACT.Identity,
                         bias=b_fox[0:8, 0:1]))
            W.wait_released(W.g - 1)
            L(af(fz[0:8, 1, :], fz[0:8, 0, :], ACT.Abs))
            L(af(fz[0:8, 1, :], fz[0:8, 1, :], ACT.Exp, scale=-1.0))
            af(fz[0:8, 1, :], fz[0:8, 1, :], ACT.Ln, bias=eps[0:8, 1:2]).then_inc(gla_act, 1)
            for h in range(8):
                s = W.arrive()
                W.release(af(sv(Hf[:, h, :], TALL), ps(s, TALL), ACT.Copy))
            for m in range(4):
                if m % 2 == 0:
                    next_hi()
                s = W.arrive()
                W.release(af(sv(pc[:, m, :], TALL), ps(s, TALL), ACT.Copy))
            for _ in range(4):
                next_hi()
                W.skip(2)
            for m in range(4):
                if m % 2 == 0:
                    next_hi()
                s = W.arrive()
                W.release(af(sv(k2[:, m, :], TALL), ps(s, TALL), ACT.Copy))
            for m in range(4):
                if m % 2 == 0:
                    next_hi()
                evac(q2[:, m, :])
            for c0 in (0, 256):
                next_hi()
                for t in range(5):
                    n = P if t < 4 else META
                    evac(v2[0:n, t, c0:c0 + 256], src=lambda s: PS[0:n, s, 0, 0:256])
            combos2 = [(i, h) for i in range(NTOK) for h in range(8)]
            attention(combos2, lambda i: META + P * (i + 1), lg2, pr2, 0.125, pT2, True,
                      lambda i, h: ya2[64 * (h % 2):64 * (h % 2) + 64, h // 2, P * i:P * i + P],
                      lambda s, h: PS[64 * (h % 2):64 * (h % 2) + 64, s, 0, 0:P])
            n_["yl"] += 8
            merge([ya2[:, k, :] for k in range(4)] + [yc2[:, k, :] for k in range(4)], YH2, sg2, 2, None)
            merged_split()
            for _ in range(4):
                next_hi()
            W.skip(8)
            norm(SEQ, split=False)
            norm(SEQ)
            swiglu(FF_UNITS, SEQ, last=True)
            norm(SEQ, split=False)
            for t in range(NTOK):
                for half in range(2):
                    s = W.arrive()
                    ins = af(o_tok[:, t, 512 * half:512 * half + 512], ps(s), ACT.Copy)
                    W.release(ins)
                    W.wait_released(W.g - 1)
                    act.sem_inc(o_ready, 1)

        @block.vector
        def _(dve):
            W = PsumWalk(dve, ready, free)
            L = Link(dve, dve_link)
            v_ = nc.vector
            tt, ts, stt = v_.tensor_tensor, v_.tensor_scalar, v_.scalar_tensor_tensor
            n_ = {"hh": 0, "mod": 0, "hn": 0, "p": 0, "y": 0}

            def ps(s, T=SEQ):
                return PS[:, s, 0, 0:T] if T <= 512 else PS[:, s, 0:2, 0:T // 2]

            def sv(ap, T):
                return ap if T <= 512 else ap.rearrange("p (b n) -> p b n", b=2)

            def h_lo(T):
                for k in range(KT):
                    n_["hh"] += 1
                    dve.wait_ge(hh_ready, n_["hh"])
                    tt(HL[:, k, 0:T], Hf[:, k, 0:T], HH[:, k, 0:T].bitcast(F32), ALU.subtract).then_inc(hl_ready, 1)

            def norm(T, src, gain, post=None):
                for k in range(KT):
                    tt(Hf[:, k, 0:T], src(k), src(k), ALU.mult).then_inc(sq_ready, 1)
                W.wait_released(W.g)
                W.skip()
                L(v_.reciprocal(rs[:, 0:T], rs[:, 0:T]))
                for k in range(KT):
                    ins = stt(Hf[:, k, 0:T], src(k), gain(k), rs[:, 0:T], ALU.mult, ALU.mult)
                    if post is None:
                        ins.then_inc(hraw_ready, 1)
                    else:
                        L.mark(ins)
                if post is not None:
                    L.wait()
                    for k in range(KT):
                        L.mark(tt(post(k), post(k), Hf[:, k, 0:T], ALU.add))
                    L.wait()
                else:
                    h_lo(T)

            def mod_products():
                n = n_["mod"]
                dve.wait_ge(mod_in[n % 2], 16 * (n // 2 + 1))
                o = macc[:, n % 2, :]
                L(ts(o, mod_raw[:, n % 2, 0, :], c_act[:, 0:1], None, ALU.mult))
                for k in range(1, KT - 1):
                    L(stt(o, mod_raw[:, n % 2, k, :], c_act[:, k:k + 1], o, ALU.mult, ALU.add))
                stt(o, mod_raw[:, n % 2, KT - 1, :], c_act[:, KT - 1:KT], o, ALU.mult, ALU.add).then_inc(macc_ready, 1)
                dve.wait_ge(macc_ready, n + 1)
                dve.sem_inc(mod_used, 1)
                n_["mod"] += 1

            def mod_evac(n):
                s = W.arrive()
                W.release(tt(modc[:, 2 * n:2 * n + 2], PS[:, s, 0, 0:2], C1[:, 2 * n:2 * n + 2], ALU.add))

            W.skip(KT)
            s = W.arrive()
            W.release(v_.tensor_copy(C1[:, 0:V1_ROWS], PS[:, s, 0, 0:V1_ROWS]))
            W.wait_released(W.g - 1)
            dve.sem_inc(cols_ready, 1)
            s = W.arrive()
            W.release(v_.tensor_copy(C2[:, 0:V2_ROWS], PS[:, s, 0, 0:V2_ROWS]))
            W.skip(1)
            s = W.arrive()
            L.mark(v_.tensor_copy(dist_sb[0:4, 0:512], PS[0:4, s, 0, :]))
            W.release(v_.tensor_copy(dist_sb[0:4, 512:640], PS[0:4, s, 1, 0:128]))
            W.wait_released(W.g - 1)
            dve.sem_inc(dist_ready, 1)
            dve.wait_ge(consts, 8)
            L.mark(v_.tensor_copy(tri2[0:64, :], tri[0:64, 0:64]))
            L.mark(v_.tensor_copy(tri2[64:128, :], tri[64:128, 64:128]))
            qn = V1["dsa_qnorm_g"]
            L(ts(eps[:, 2:3], C1[:, qn:qn + 1], float(P) ** -0.5, None, ALU.mult))
            dve.wait_ge(cact_ready, 1)
            for n in range(MOD1):
                mod_products()
                if n >= 1:
                    mod_evac(n - 1)
            mod_evac(MOD1 - 1)
            W.wait_released(W.g - 1)

            def adaptive_gain(dst, sc0, g0):
                L(stt(dst[:, :], modc[:, sc0:sc0 + KT], 1.0, C1[:, g0:g0 + KT], ALU.add, ALU.mult))

            adaptive_gain(gain1, 8, V1["g_norm1"])
            W.wait_released(10)
            norm(SEQ, lambda k: R[:, k, META:TALL], lambda k: gain1[:, k:k + 1])
            W.skip(3)

            L(ts(keep0[:, :], outside[:, :], 0.0, BIG, ALU.is_ge, ALU.mult))
            rounds = [(i, r) for i in (1, 2, 3) for r in range(TOPK // 8)]
            done_mods = MOD1
            for n, (kind, _) in enumerate(P1):
                now = MODS_AT[n]
                for _ in range(now):
                    mod_products()
                W.skip(2 if kind == "fm" else NTOK)
                if n == 0:
                    for x in range(12):
                        i, h = x // 4 + 1, x % 4
                        w = (i + 1) * P
                        W.wait_released(W.g)
                        W.skip()
                        src = relu_s[:, x % 2, 0:w]
                        col = iw[:, i, h:h + 1]
                        if h == 0:
                            ins = ts(sc[i][:, :], src, col, 0.0, ALU.mult, ALU.add)
                        else:
                            ins = stt(sc[i][:, :], src, col, sc[i][:, :], ALU.mult, ALU.add)
                        ins.then_inc(relu_used, 1)
                        dve.wait_ge(relu_used, x + 1)
                        if h == 3:
                            L(tt(sc[i][:, i * P:w], sc[i][:, i * P:w], outside[:, :], ALU.add))
                if n >= 1:
                    for i, r in rounds[4 * (n - 1):4 * n]:
                        L(v_.max(max8[:, :], sc[i][:, :]))
                        L(v_.match_replace(sc[i][:, :], max8[:, :], sc[i][:, :], REPLACED))
                        if r == TOPK // 8 - 1:
                            L(ts(sc[i][:, :], sc[i][:, :], REPLACED, BIG, ALU.is_equal, ALU.mult))
                for _ in range(now):
                    mod_evac(done_mods)
                    done_mods += 1

            W.wait_released(W.g - 1)
            dve.wait_ge(gm_in, 64)
            for t in range(NTOK):
                L.mark(v_.bn_stats(stats[:, t, :], v[:, t, :]))
            L.wait()
            for t in range(NTOK):
                ins = v_.bn_aggr(mv[:, t, :], stats[:, t, :])
            ins.then_inc(var_ready, 1)
            W.wait_released(W.g)
            W.skip()
            tt(wsT[:, :, :], wsT[:, :, :], tri[:, :].unsqueeze(1).to_broadcast([P, 4, P]), ALU.mult).then_inc(wsT_ready, 1)
            dve.wait_ge(std_ready, 1)
            dve.wait_ge(var_ready, 1)
            L(v_.reciprocal(rstd[:, :], rstd[:, :]))
            for t in range(NTOK):
                L.mark(ts(v[:, t, :], v[:, t, :], mv[:, t, 0:1], rstd[:, t:t + 1], ALU.subtract, ALU.mult))
            L.wait()
            for t in range(NTOK):
                L.mark(tt(v[:, t, :], v[:, t, :], ln_rows[:, 0, :], ALU.mult))
            L.wait()
            for t in range(NTOK):
                ins = tt(v[:, t, :], v[:, t, :], ln_rows[:, 1, :], ALU.add)
            ins.then_inc(gmv_ready, 1)
            for g in range(4):
                s = W.arrive()
                m = mixt[:, g % 2, :]
                W.release(tt(m.rearrange("p (t n) -> p t n", t=NTOK), PS[:, s, 0, :].rearrange("p (t n) -> p t n", t=NTOK),
                             bs_rows[:, g, :].unsqueeze(1).to_broadcast([P, NTOK, P]), ALU.add))
                W.wait_released(W.g - 1)
                ins = tt(u[:, g, :], u[:, g, :], m, ALU.mult)
                L.mark(ins)
            L.wait()
            dve.sem_inc(gmlp_done, 1)

            def head_norms(items):
                for x in range(len(items) + 1):
                    if x < len(items):
                        src, gain, before, after = items[x]
                        if before:
                            before()
                        tt(sqh[:, (n_["hn"] + x) % 2, :], src, src, ALU.mult).then_inc(hsq_ready, 1)
                    if x >= 1:
                        src, gain, before, after = items[x - 1]
                        r = rsh[:, (n_["hn"] + x - 1) % 2, :]
                        W.wait_released(W.g)
                        W.skip()
                        L(v_.reciprocal(r, r))
                        stt(src, src, gain, r, ALU.mult, ALU.mult).then_inc(hn_done, 1)
                        if after:
                            dve.wait_ge(hn_done, n_["hn"] + x)
                            after()
                n_["hn"] += len(items)

            kn = V1["dsa_knorm_g"]
            head_norms([(dq[:, h, :], eps[:, 2:3], None, None) for h in range(4)] +
                       [(dk[:, h, :], C1[:, kn:kn + 1], None, None) for h in range(4)])

            def attention(combos, logits, pr, scale, width):
                N = len(combos)
                for n in range(N + 3):
                    if n < N:
                        i, h = combos[n]
                        c = n % 32
                        logits(n % 2, i, h, nmax[:, c:c + 1])
                        ts(nmax[:, c:c + 1], nmax[:, c:c + 1], -scale, None, ALU.mult).then_inc(lg_ready, 1)
                    if 0 <= n - 1 < N:
                        i, h = combos[n - 1]
                        c = (n - 1) % 32
                        n_["p"] += 1
                        dve.wait_ge(p_ready, n_["p"])
                        L(v_.reciprocal(rden[:, c:c + 1], den[:, c:c + 1]))
                        p = pr[:, (n - 1) % 3, 0:width(i)]
                        ts(p, p, rden[:, c:c + 1], None, ALU.mult).then_inc(pn_ready, 1)
                    if 0 <= n - 2 < N:
                        W.skip(1)
                    if 0 <= n - 3 < N:
                        W.skip(1)

            def dsa_logits(par, i, h, top):
                w = (i + 1) * P
                L(stt(bm[:, 0:w], keep[i][:, :], -BIG, bias_rev[:, h, 0:w][:, ::-1], ALU.add, ALU.add))
                s = W.arrive()
                W.release(v_.tensor_tensor_reduce(lg1[:, par, 0:w], PS[:, s, 0, 0:w], bm[:, 0:w], 1.0, -3.0e38, ALU.add, ALU.max, top))
                W.wait_released(W.g - 1)

            dve.wait_ge(bias_in, 64)
            combos1 = [(i, h) for i in range(NTOK) for h in range(4)]
            attention(combos1, dsa_logits, pr1, 1.0, lambda i: (i + 1) * P)

            def chunks(ap):
                return ap.rearrange("p (c t) -> p c t", t=CHUNK)

            dve.wait_ge(gla_act, 1)
            L(v_.memset(t2[:, :], 1.0))
            L(v_.memset(chunks(t2[:, :])[:, :, 0:1], 0.0))
            L.mark(v_.memset(Kp[:, :, :], 0.0))
            L.mark(v_.memset(Qp[:, :, :], 0.0))
            for j in range(2):
                W.skip(1)
                tj = (t0, t1)[j]
                dve.wait_ge(gla_act, j + 1)
                L(stt(tj[:, :], Bc[:, j, :], 0.0, tj[:, :], ALU.min, ALU.subtract))
                L(v_.tensor_tensor_scan(Bc[:, j, :], t2[:, :], tj[:, :], 0.0, ALU.mult, ALU.add))
            for j in range(2):
                L.mark(v_.tensor_copy(ebl[:, j, :], chunks(Bc[:, j, :])[:, :, CHUNK - 1:CHUNK].rearrange("p c t -> p (c t)")))
            L.wait()
            seq = 0
            tb = (t0, t1, t2)
            taken = []
            for j in range(2):
                Bj = Bc[:, j, :]
                for x in range(8):
                    if x < 7:
                        b = tb[(seq + x) % 3][:, :]
                        if seq + x >= 3:
                            L.wait(taken[seq + x - 3])
                        if x == 0:
                            ins = v_.tensor_copy(b, Bj)
                        elif x == 1:
                            ins = tt(chunks(b), chunks(Bj)[:, :, CHUNK - 1:CHUNK].to_broadcast([P, 8, CHUNK]), chunks(Bj), ALU.subtract)
                        elif x == 2:
                            subs = Bj.rearrange("p (c t) -> p c t", t=SUB)
                            ins = tt(b.rearrange("p (c t) -> p c t", t=SUB), subs[:, :, SUB // 2 - 1:SUB // 2].to_broadcast([P, SEQ // SUB, SUB]),
                                     subs, ALU.subtract)
                        else:
                            q = x - 3
                            pv = SUB * q + SUB // 2 - 1
                            ins = tt(chunks(b)[:, :, SUB * q:CHUNK], chunks(Bj)[:, :, SUB * q:CHUNK],
                                     chunks(Bj)[:, :, pv:pv + 1].to_broadcast([P, 8, CHUNK - SUB * q]), ALU.subtract)
                        ins.then_inc(exp_arg, 1)
                    if x >= 1:
                        y = x - 1
                        b = tb[(seq + y) % 3][:, :]
                        dve.wait_ge(gla_act, 2 + seq + y + 1)
                        if y == 0:
                            L.mark(stt(qe[:, j, :], gq[:, j, :], 0.125, b, ALU.mult, ALU.mult))
                        elif y == 1:
                            L.mark(tt(kk[:, j, :], gk[:, j, :], b, ALU.mult))
                        elif y == 2:
                            for q in range(4):
                                cs = slice(SUB * q, SUB * q + SUB)
                                L.mark(tt(chunks(Kp[:, q, :])[:, :, cs], chunks(gk[:, j, :])[:, :, cs], chunks(b)[:, :, cs], ALU.mult))
                        else:
                            q = y - 3
                            cs = slice(SUB * q, CHUNK)
                            L.mark(stt(chunks(Qp[:, q, :])[:, :, cs], chunks(gq[:, j, :])[:, :, cs], 0.125, chunks(b)[:, :, cs], ALU.mult, ALU.mult))
                        taken.append(L.n)
                seq += 7
                L.wait()
                dve.sem_inc(gla_dve, 1)
                for hh in range(2):
                    s = W.arrive()
                    W.release(tt(attT[:, 2 * j + hh, :, :], PS[:, s, 0, 0:256].rearrange("p (c t) -> p c t", t=CHUNK),
                                 tri2[:, :].unsqueeze(1).to_broadcast([P, NTOK, CHUNK]), ALU.mult))
                W.skip(1)
            W.wait_released(W.g - 2)
            dve.sem_inc(exp_arg, 1)
            dve.wait_ge(gla_act, 2 + seq + 1)
            for c in range(7):
                s = W.arrive()
                if c == 0:
                    ins = v_.tensor_copy(Sall[:, 1, :, :], PS[:, s, 0, 0:256].rearrange("p (j e) -> p j e", j=2))
                else:
                    L(stt(Sall[:, c + 1, 0, :], Sall[:, c, 0, :], ebl[:, 0, c:c + 1], PS[:, s, 0, 0:P], ALU.mult, ALU.add))
                    ins = stt(Sall[:, c + 1, 1, :], Sall[:, c, 1, :], ebl[:, 1, c:c + 1], PS[:, s, 0, P:2 * P], ALU.mult, ALU.add)
                W.release(ins)
                W.wait_released(W.g - 1)
            dve.sem_inc(gla_dve, 1)
            gn = V1["gla_norm_g"]
            g0 = W.g
            W.skip(4)
            head_norms([(og[:, h, :], C1[:, gn:gn + 1], (lambda g=g0 + h: W.wait_released(g)),
                         (lambda h=h: L.mark(tt(gr[:, h, :], gr[:, h, :], og[:, h, :], ALU.mult)))) for h in range(4)])
            L.wait()

            def merge(srcs, yh, yl, sg_, mt, n_br):
                dve.sem_inc(y_src, 1)
                for k in range(KT):
                    L.mark(v_.memset(Hf[:, k, 0:SEQ], 0.0))
                L.wait()
                for n, y in enumerate(srcs):
                    n_["y"] += 1
                    dve.wait_ge(yh_ready, n_["y"])
                    tt(yl[:, n, :], y, yh[:, n, :].bitcast(F32), ALU.subtract).then_inc(yl_ready, 1)
                for mq in range(2):
                    g0 = W.g

                    def body():
                        W.skip(4)
                        for m in range(4):
                            s = W.arrive()
                            W.wait_released(W.g - 4)
                            W.release(tt(mt[:, m % 2, :], ps(s), sg_[:, m, :], ALU.mult))
                            W.wait_released(W.g - 1)
                            h = Hf[:, 4 * mq + m, 0:SEQ]
                            L(tt(h, h, mt[:, m % 2, :], ALU.add))

                    body()
                    with dve.Fori(0, n_br - 1) as i:
                        W.g = g0 + 8
                        W.more, L.more = i * 2, i * 4
                        body()
                    W.g = g0 + 8 * n_br
                    W.more = L.more = 0
                    L.n += 4 * (n_br - 2)
                dve.sem_inc(merged_ready, 1)
                h_lo(SEQ)

            merge([u[:, k, :] for k in range(4)] + [gr[:, k, :] for k in range(4)] + [dq[:, k, :] for k in range(4)],
                  YH, YL, sg1, mt1, 3)
            for m in range(KT):
                s = W.arrive()
                W.release(stt(R[:, m, META:TALL], ps(s), modc[:, 16 + m:17 + m], R[:, m, META:TALL], ALU.mult, ALU.add))
            adaptive_gain(gain2, 32, V1["g_norm2"])
            W.wait_released(W.g - 1)
            W.wait_released(W.g - 2)
            W.wait_released(W.g - 3)
            W.wait_released(W.g - 4)
            norm(SEQ, lambda k: R[:, k, META:TALL], lambda k: gain2[:, k:k + 1])

            s = W.arrive()
            W.release(tt(rl[:, :, :], PS[:, s, 0, 0:80].rearrange("p (t c) -> p t c", c=20),
                         b_route[:, 0:20].unsqueeze(1).to_broadcast([P, NTOK, 20]), ALU.add))
            W.wait_released(W.g - 1)

            def r(n, a_=0, b_=4):
                return rt[:, n, :, a_:b_]

            def bc(ap):
                return ap.to_broadcast([P, NTOK, 4])

            def first_of(dst, eq, seen):
                L(v_.tensor_copy(r(dst, 0, 1), r(eq, 0, 1)))
                L(v_.tensor_copy(r(seen, 0, 1), r(eq, 0, 1)))
                for c in range(1, 4):
                    L(ts(r(dst, c, c + 1), r(seen, c - 1, c), -1.0, 1.0, ALU.mult, ALU.add))
                    L(tt(r(dst, c, c + 1), r(dst, c, c + 1), r(eq, c, c + 1), ALU.mult))
                    L(tt(r(seen, c, c + 1), r(seen, c - 1, c), r(dst, c, c + 1), ALU.add))

            gl = rl[:, :, 0:4]
            L(v_.tensor_reduce(r(1, 0, 1), gl, AX, ALU.max))
            L(tt(r(2), gl, bc(r(1, 0, 1)), ALU.is_equal))
            first_of(3, 2, 4)
            L(tt(r(0), gl, bc(r(1, 0, 1)), ALU.subtract))
            L(tt(r(5), rl[:, :, 4:8], bc(r(3, 0, 1)), ALU.mult))
            for gi in range(1, 4):
                L(tt(r(6), rl[:, :, 4 + 4 * gi:8 + 4 * gi], bc(r(3, gi, gi + 1)), ALU.mult))
                L(tt(r(5), r(5), r(6), ALU.add))
            L(v_.tensor_reduce(r(7, 0, 1), r(5), AX, ALU.max))
            L(tt(r(2), r(5), bc(r(7, 0, 1)), ALU.is_equal))
            first_of(8, 2, 4)
            L(stt(r(9), r(8), -BIG, r(5), ALU.mult, ALU.add))
            L(v_.tensor_reduce(r(7, 1, 2), r(9), AX, ALU.max))
            L(tt(r(2), r(9), bc(r(7, 1, 2)), ALU.is_equal))
            first_of(10, 2, 4)
            L(tt(r(15, 0, 1), r(7, 1, 2), r(7, 0, 1), ALU.subtract))
            dve.sem_inc(ex_ready, 1)
            dve.wait_ge(ex_done, 1)
            L(v_.tensor_reduce(r(11, 0, 1), r(0), AX, ALU.add))
            L(v_.reciprocal(r(11, 1, 2), r(11, 0, 1)))
            L(ts(r(12, 0, 1), r(15, 0, 1), 1.0, None, ALU.add))
            L(v_.reciprocal(r(12, 1, 2), r(12, 0, 1)))
            L(tt(r(12, 2, 3), r(12, 1, 2), r(11, 1, 2), ALU.mult))
            L(tt(r(12, 3, 4), r(12, 2, 3), r(15, 0, 1), ALU.mult))
            L(tt(r(13), r(8), bc(r(12, 2, 3)), ALU.mult))
            L(tt(r(14), r(10), bc(r(12, 3, 4)), ALU.mult))
            L(tt(r(13), r(13), r(14), ALU.add))
            for gi in range(4):
                L(tt(rc[:, :, 4 * gi:4 * gi + 4], r(13), bc(r(3, gi, gi + 1)), ALU.mult))
            dve.sem_inc(router_done, 1)
            W.wait_made(W.g)
            W.skip(1)
            W.skip(N_EXP)

            units_done = {"n": 0}

            def swiglu(units, T, weight=None):
                for k in range(KT):
                    L.mark(v_.memset(yacc[:, k, 0:T], 0.0))
                L.wait()
                base = units_done["n"]

                def up(n, par, more=0):
                    W.skip(2)
                    for m in range(2):
                        s = W.arrive()
                        W.wait_released(W.g - 2)
                        f = actf[:, m, 0:T]
                        W.release(tt(sv(f, T), ps(s, T), sv(sg[:, m, 0:T], T), ALU.mult))
                        W.wait_released(W.g - 1)
                        if weight is not None:
                            L(tt(f, f, weight(n), ALU.mult))
                        L(v_.tensor_copy(ah[:, par, m, 0:T], f))
                        ins = tt(al[:, par, m, 0:T], f, ah[:, par, m, 0:T].bitcast(F32), ALU.subtract)
                        if m == 1:
                            ins.then_inc(moe_act, 1)

                def down():
                    for m in range(KT):
                        s = W.arrive()
                        y = sv(yacc[:, m, 0:T], T)
                        W.release(tt(y, y, ps(s, T), ALU.add))

                up(0, 0)
                pairs = (units - 1) // 2
                g0, l0 = W.g, L.n
                per = 4 if weight is None else 8
                with dve.Fori(0, pairs) as i:
                    W.g, L.n = g0, l0
                    W.more, L.more = i * 6, i * per
                    for par in range(2):
                        up(i * 2 + (par + 1), 1 - par, i * 2)
                        down()
                W.g, L.n = g0 + 24 * pairs, l0 + per * pairs
                W.more = L.more = 0
                for n in range(2 * pairs, units):
                    if n + 1 < units:
                        up(n + 1, (n + 1) % 2)
                    down()
                units_done["n"] += units
                for b in range(1, 5):
                    W.wait_released(W.g - b)

            def routing(n):
                if isinstance(n, int):
                    return comb[:, n, :]
                return comb[:, bass.ds(n, 1), :].rearrange("p a n -> p (a n)")

            for b in range(1, 5):
                W.wait_released(W.g - b)
            swiglu(N_EXP, SEQ, routing)
            for m in range(KT):
                L.mark(stt(R[:, m, META:TALL], yacc[:, m, 0:SEQ], modc[:, 40 + m:41 + m], R[:, m, META:TALL], ALU.mult, ALU.add))
            L.wait()

            def c2(n):
                return lambda k: C2[:, 8 * n + k:8 * n + k + 1]

            L.mark(ts(gain1[:, :], C2[:, 8:16], 0.5, None, ALU.mult))
            L.mark(ts(gain2[:, :], C2[:, 40:48], 0.5, None, ALU.mult))
            L.wait()
            every = lambda k: R[:, k, 0:TALL]
            real = lambda k: R[:, k, META:TALL]
            norm(TALL, every, c2(0))
            swiglu(FF_UNITS, TALL)
            norm(TALL, lambda k: yacc[:, k, 0:TALL], lambda k: gain1[:, k:k + 1], post=every)
            norm(TALL, every, c2(2))
            W.skip(1)
            dve.wait_ge(gla_act, 2 + seq + 1 + 1)
            L(stt(fz[0:8, 1, :], fz[0:8, 0, :], 0.0, fz[0:8, 1, :], ALU.min, ALU.subtract))
            L(v_.memset(fz[0:8, 0, :], 1.0))
            L(v_.tensor_tensor_scan(negF[0:8, :], fz[0:8, 0, :], fz[0:8, 1, :], 0.0, ALU.mult, ALU.subtract))
            L(ts(negF[0:8, :], negF[0:8, :], float(8), None, ALU.mult))
            dve.sem_inc(negF_ready, 1)
            f0 = W.g
            W.skip(8)
            W.skip(4)
            for m in range(4):
                s = W.arrive()
                W.wait_released(W.g - 4)
                W.release(tt(sv(pc[:, m, :], TALL), ps(s, TALL), sv(pc[:, m, :], TALL), ALU.mult))
                W.wait_released(W.g - 1)
                for j in range(3):
                    src, w = pc[:, m, META - 2 + j:META - 2 + j + SEQ], C2[:, CONV_ROW + 4 * j + m:CONV_ROW + 4 * j + m + 1]
                    if j == 0:
                        L(ts(yc2[:, m, :], src, w, None, ALU.mult))
                    else:
                        L(stt(yc2[:, m, :], src, w, yc2[:, m, :], ALU.mult, ALU.add))
            for m in range(4):
                s = W.arrive()
                W.release(tt(yc2[:, m, :], ps(s), yc2[:, m, :], ALU.mult))
            W.skip(4 + 4 + 10)

            def fox_logits(par, i, h, top):
                s = W.arrive()
                row = lg2[:, par, :]
                d0 = META + P * i
                n0 = min(512, d0 + P)
                if d0 + P > n0:
                    L.mark(tt(row[:, 512:TALL], PS[:, s, 1, 0:TALL - 512], Hf[:, h, 512:TALL], ALU.add))
                W.release(tt(row[:, 0:n0], PS[:, s, 0, 0:n0], Hf[:, h, 0:n0], ALU.add))
                W.wait_released(W.g - 1)
                L(tt(row[:, d0:d0 + P], row[:, d0:d0 + P], outside[:, :], ALU.add))
                L(v_.tensor_reduce(top, row[:, 0:d0 + P], AX, ALU.max))

            for b in range(1, 9):
                W.wait_released(f0 + 8 - b)
            combos2 = [(i, h) for i in range(NTOK) for h in range(8)]
            attention(combos2, fox_logits, pr2, 0.125, lambda i: META + P * (i + 1))
            W.wait_released(W.g - 1)
            merge([ya2[:, k, :] for k in range(4)] + [yc2[:, k, :] for k in range(4)], YH2, YL2, sg2, mt2, 2)
            for m in range(KT):
                s = W.arrive()
                W.release(v_.tensor_copy(yacc[:, m, 0:SEQ], ps(s)))
            for b in range(1, 5):
                W.wait_released(W.g - b)
            norm(SEQ, lambda k: yacc[:, k, 0:SEQ], c2(3), post=real)
            norm(SEQ, real, c2(4))
            swiglu(FF_UNITS, SEQ)
            norm(SEQ, lambda k: yacc[:, k, 0:SEQ], lambda k: gain2[:, k:k + 1], post=real)
            dve.sem_inc(r_done, 1)


_OUT = (1, SEQ, D)
_INS = ["x", "c", "w_mod", "b_mod", "g_norm1", "g_norm2", "w_in", "gmlp_ln_g", "gmlp_ln_b", "gmlp_w_s", "gmlp_b_s",
        "gla_w_gate2", "gla_b_gate", "gla_norm_g", "dsa_qnorm_g", "dsa_knorm_g", "rel_bias", "w_branch",
        "b_branch_gate", "w_out", "w_group", "b_group", "w_router", "b_router", "w_exp_gate", "w_exp_up",
        "w_exp_down", "meta_tokens_2", "w_in_2", "b_forget_2", "conv_w_2", "w_attn_branch_2", "w_conv_branch_2",
        "w_out_2", "g_ffn1_pre_2", "g_ffn1_post_2", "w_ffn1_in_2", "w_ffn1_out_2", "g_mix_pre_2", "g_mix_post_2",
        "g_ffn2_pre_2", "g_ffn2_post_2", "w_ffn2_in_2", "w_ffn2_out_2"]


def kernel(**inputs):
    import numpy as _np
    import concourse.bacc as _bacc
    from concourse import mybir as _mybir
    from concourse.bass_utils import run_bass_kernel_spmd as _run

    nc = _bacc.Bacc("TRN2", target_bir_lowering=False, num_devices=1, dynamic_dma_scratch_size=1024)
    arrays, args = {}, {}
    for name in _INS:
        x = _np.ascontiguousarray(inputs[name])
        arrays[f"in_{name}"] = x
        args[name] = nc.dram_tensor(f"in_{name}", x.shape, _mybir.dt.from_np(x.dtype), kind="ExternalInput").ap()
    arrays["one_hot"] = distance_buckets()
    one_hot = nc.dram_tensor("one_hot", (32, 640), _mybir.dt.float32, kind="ExternalInput").ap()
    out = nc.dram_tensor("out_0", _OUT, _mybir.dt.float32, kind="ExternalOutput").ap()
    build(nc, args, one_hot, out)
    r = _run(nc, [arrays], core_ids=[0])
    return r.results[0]["out_0"]
```

```python
from contextlib import ExitStack

import numpy as np
import concourse.bass as bass
from concourse import mybir

F32 = mybir.dt.float32
F32R = mybir.dt.float32r
ALU = mybir.AluOpType
ACT = mybir.ActivationFunctionType
AX = mybir.AxisListType.X

P = 128
D = 1024
SQ_OWN = 3
KT = D // P
SEQ = 512
META = 16
TALL = SEQ + META
NTOK = SEQ // P
DB = 512
BT = DB // P
EPS = 1e-6
RING = 3
CH = 2048
SLOTS = 4
TOPK = 128
REPLACED = -3.0e38
OUTSIDE = -3.3e38
BIG = 1e30
N_EXP = 16
CHUNK = 64
SUB = 16
D_FF = 2816
FF_UNITS = D_FF // 256

(A_U, A_V, G_Q, G_K, G_V, G_R, G_A, D_Q, D_K, D_V, D_IQ, D_IK, D_IW, GATES) = np.cumsum(
    [0, 512, 512, 256, 256, 512, 512, 16, 512, 512, 512, 256, 64, 4]).tolist()
(Q2, K2, V2, F2, CB2, CC2, CI2, GA2, GC2) = np.cumsum([0, 512, 512, 512, 8, 512, 512, 512, 1024]).tolist()

V1 = dict(b_mod=0, c=48, g_norm1=56, g_norm2=64, b_branch_gate=72, gla_b_gate=96, gla_norm_g=98,
          dsa_qnorm_g=99, dsa_knorm_g=100)
V1_ROWS = 101
V2_NAMES = ["g_ffn1_pre_2", "g_ffn1_post_2", "g_mix_pre_2", "g_mix_post_2", "g_ffn2_pre_2", "g_ffn2_post_2"]
CONV_ROW = 48
V2_ROWS = 60


def distance_buckets():
    n = np.maximum(np.arange(640) - 127, 0)
    large = 16 + (np.log(np.maximum(n, 16).astype(np.float32) / 16) / np.float32(np.log(8.0)) * 16).astype(np.int32)
    b = np.where(n < 16, n, np.minimum(large, 31))
    return (np.arange(32)[:, None] == b[None, :]).astype(np.float32)


class PsumWalk:

    def __init__(self, eng, ready, free):
        self.eng, self.ready, self.free = eng, ready, free
        self.g = 0
        self.more = 0

    def claim(self):
        if self.g >= SLOTS:
            self.eng.wait_ge(self.free[self.g % SLOTS], self.g // SLOTS + self.more)
        return self.g % SLOTS

    def made(self, ins):
        ins.then_inc(self.ready[self.g % SLOTS], 1)
        self.g += 1

    def arrive(self):
        self.eng.wait_ge(self.ready[self.g % SLOTS], self.g // SLOTS + 1 + self.more)
        return self.g % SLOTS

    def release(self, ins):
        ins.then_inc(self.free[self.g % SLOTS], 1)
        self.g += 1

    def skip(self, n=1):
        self.g += n

    def wait_released(self, g):
        self.eng.wait_ge(self.free[g % SLOTS], g // SLOTS + 1 + self.more)

    def wait_made(self, g):
        self.eng.wait_ge(self.ready[g % SLOTS], g // SLOTS + 1 + self.more)


class Link:

    def __init__(self, eng, sem):
        self.eng, self.sem, self.n, self.more = eng, sem, 0, 0

    def mark(self, ins):
        self.n += 1
        ins.then_inc(self.sem, 1)
        return self.n

    def wait(self, n=None):
        self.eng.wait_ge(self.sem, (self.n if n is None else n) + self.more)

    def __call__(self, ins):
        self.mark(ins)
        self.wait()


def token_groups(T):
    return (P, T // P) if T <= 512 else (T // 6, 6)


def halves(T):
    return [(0, T)] if T <= 512 else [(0, T // 2), (T // 2, T // 2)]


def build(nc, a, one_hot, out):
    with ExitStack() as ctx:
        BASE = 1280
        names = {}

        def at(name, off, shape, dt=F32):
            names[name] = off
            return nc.alloc_sbuf_tensor_at(name, [P] + list(shape), dt, offset=off)

        def sem(name):
            return ctx.enter_context(nc.semaphore(name))

        PS = ctx.enter_context(nc.psum_tensor("PS", [P, SLOTS, 2, 512], F32))

        B = BASE
        w_raw = at("w_raw", B, [RING, CH]); B += RING * CH * 4
        w_hi = at("w_hi", B, [RING, CH], F32R); B += RING * CH * 4
        w_lo = at("w_lo", B, [RING, CH], F32R); B += RING * CH * 4
        R = at("R", B, [KT, TALL]); B += KT * TALL * 4
        HF_OFF = B
        Hf = at("Hf", B, [KT, TALL]); B += KT * TALL * 4
        HH_AT = B
        HH = at("HH", B, [KT, TALL], F32R); B += KT * TALL * 4
        HL_AT = B
        HL = at("HL", B, [KT, TALL], F32R); B += KT * TALL * 4
        ident = at("ident", B, [P]); B += 512
        ones = at("ones", B, [P]); B += 512
        tri = at("tri", B, [P]); B += 512
        outside = at("outside", B, [P]); B += 512
        C1 = at("C1", B, [P]); B += 512
        C2 = at("C2", B, [P]); B += 512
        modc = at("modc", B, [48]); B += 192
        w_route = at("w_route", B, [KT, 20]); B += 640
        w_forget = at("w_forget", B, [KT, 8]); B += 256
        w_gate2 = at("w_gate2", B, [256]); B += 1024
        rs = at("rs", B, [TALL]); B += TALL * 4
        c_act = at("c_act", B, [KT]); B += 32
        iw = at("iw", B, [NTOK, 4]); B += 64
        b_fox = at("b_fox", B, [8]); B += 32
        relb = at("relb", B, [4]); B += 32
        eps = at("eps", B, [8]); B += 32
        gain1 = at("gain1", B, [KT]); B += 32
        gain2 = at("gain2", B, [KT]); B += 32
        tri2 = at("tri2", B, [CHUNK]); B += 256
        nmax = at("nmax", B, [32]); B += 128
        den = at("den", B, [32]); B += 128
        rden = at("rden", B, [32]); B += 128
        stats = at("stats", B, [NTOK, 6]); B += 96
        mv = at("mv", B, [NTOK, 2]); B += 32
        rstd = at("rstd", B, [NTOK]); B += 32
        ebl = at("ebl", B, [2, 8]); B += 64
        b_route = at("b_route", B, [32]); B += 128
        rsc = at("rsc", B, [32]); B += 128
        A0 = B
        room = nc.sbuf_usable_end - A0

        def ar(name, off, shape, dt=F32):
            assert off + int(np.prod(shape)) * 4 <= room, (name, off, room)
            return at(name, A0 + off, shape, dt)

        def hf(name, off, shape, dt=F32):
            assert off + int(np.prod(shape)) * 4 <= KT * TALL * 4
            return at(name, HF_OFF + off, shape, dt)

        u = ar("u", 0, [BT, SEQ])
        w_small = ar("w_small", 0, [KT, 148])
        v = ar("v", 8192, [NTOK, DB])
        gq = ar("gq", 16384, [2, SEQ])
        gk = ar("gk", 20480, [2, SEQ])
        gv = ar("gv", 24576, [NTOK, DB])
        gr = ar("gr", 32768, [BT, SEQ])
        dq = ar("dq", 40960, [BT, SEQ])
        oh_sb = ar("oh_sb", 40960, [640])
        dist_sb = ar("dist_sb", 43520, [640])
        vec_a = ar("vec_a", 46080, [P])
        vec_b = ar("vec_b", 46592, [P])
        meta_sb = ar("meta_sb", 49152, [D])
        dk = ar("dk", 49152, [BT, SEQ])
        dv = ar("dv", 57344, [NTOK, DB])
        relu_s = ar("relu_s", 57344, [2, SEQ])
        iq = ar("iq", 65536, [2, SEQ])
        ik = ar("ik", 69632, [SEQ])
        sc = [None] + [ar(f"sc{i}", 71680 + (0, 1024, 2560)[i - 1], [(i + 1) * P]) for i in (1, 2, 3)]
        keep0 = ar("keep0", 76288, [P])
        ga = rs
        macc = ar("macc", 61440, [2, 256])
        max8 = ar("max8", 76800, [8])
        keep = [keep0] + sc[1:]
        x_tok = hf("x_tok", 0, [NTOK, D])
        mod_raw = hf("mod_raw", 0, [2, KT, 256])
        mod_more = at("mod_more", HH_AT, [2, KT, 256])
        squares1 = at("squares1", HL_AT, [KT, SEQ])
        ws = hf("ws", 0, [4, P])
        wsT = hf("wsT", 2048, [4, P])
        ln_rows = hf("ln_rows", 4096, [2, DB])
        bs_rows = hf("bs_rows", 8192, [4, P])
        mixt = hf("mixt", 10240, [2, SEQ])
        sqh = hf("sqh", 0, [8, SEQ])
        bias_rev = ar("bias_rev", 8192, [4, SEQ])
        lg1 = hf("lg1", 0, [2, SEQ])
        pr1 = hf("pr1", 4096, [3, SEQ])
        bm = hf("bm", 10240, [SEQ])
        pT1 = hf("pT1", 12288, [2, 4, P])
        Bc = ar("Bc", 65536, [2, SEQ])
        t0 = ar("t0", 69632, [SEQ])
        t1 = ar("t1", 71680, [SEQ])
        t2 = ar("t2", 73728, [SEQ])
        Kp = hf("Kp", 0, [4, SEQ])
        Qp = hf("Qp", 8192, [4, SEQ])
        qe = ar("qe", 8192, [2, SEQ])
        kk = ar("kk", 12288, [2, SEQ])
        kkT = ar("kkT", 49152, [2, NTOK, P])
        attT = ar("attT", 53248, [4, NTOK, CHUNK])
        og = ar("og", 57344, [4, SEQ])
        Sall = ar("Sall", 16384, [8, 2, P])
        YH = ar("YH", 8192, [12, SEQ], F32R)
        YL = ar("YL", 49152, [12, SEQ], F32R)
        sg1 = ar("sg1", 0, [4, SEQ])
        mt1 = ar("mt1", 73728, [2, SEQ])
        yacc = ar("yacc", 0, [KT, TALL])
        ah = ar("ah", 16896, [2, 2, TALL], F32R)
        al = ar("al", 25344, [2, 2, TALL], F32R)
        actf = ar("actf", 33792, [2, TALL])
        sg = ar("sg", 38016, [2, TALL])
        comb = ar("comb", 42240, [N_EXP, SEQ])
        combT = ar("combT", 75008, [SEQ])
        rl = ar("rl", 0, [NTOK, 20])
        rt = ar("rt", 1024, [16, NTOK, 4])
        rc = ar("rc", 2048 + 1024, [NTOK, 16])
        q2 = ar("q2", 0, [4, SEQ])
        k2 = ar("k2", 8192, [4, TALL])
        v2 = ar("v2", 16640, [5, DB])
        pc = ar("pc", 26880, [4, TALL])
        yc2 = ar("yc2", 35328, [4, SEQ])
        negF = ar("negF", 43520, [TALL])
        fz = ar("fz", 45632, [2, TALL])
        ya2 = ar("ya2", 49856, [4, SEQ])
        lg2 = ar("lg2", 58048, [2, TALL])
        pr2 = ar("pr2", 62272, [3, TALL])
        pT2 = ar("pT2", 68608, [2, 5, P])
        YH2 = ar("YH2", 0, [8, SEQ], F32R)
        YL2 = ar("YL2", 16384, [8, SEQ], F32R)
        sg2 = ar("sg2", 58048, [4, SEQ])
        mt2 = ar("mt2", 66240, [2, SEQ])
        o_tok = ar("o_tok", 0, [NTOK, D])

        dist_dram = nc.dram_tensor("dist_dram", (4, 640), F32, kind="Internal").ap()

        ready = [sem(f"psum_ready{s}") for s in range(SLOTS)]
        free = [sem(f"psum_free{s}") for s in range(SLOTS)]
        w_in_sem = [sem(f"chunk_landed{s}") for s in range(RING)]
        hi_done = sem("chunk_hi_done")
        split = sem("chunk_split")
        begun = sem("chunk_begun")
        vec_in = sem("vectors_in")
        x_in = sem("x_in")
        small_in = sem("small_in")
        oh_in = sem("one_hot_in")
        dist_out = sem("dist_out")
        bias_in = sem("bias_in")
        gm_in = sem("gmlp_in")
        mod_in = [sem(f"mod_landed{s}") for s in range(4)]
        mod_used = sem("mod_used")
        consts = sem("consts")
        out_done = sem("out_done")
        cols_ready = sem("columns_ready")
        dist_ready = sem("dist_ready")
        cact_ready = sem("c_act_ready")
        macc_ready = sem("macc_ready")
        sq_ready = sem("squares_ready")
        sqsum_ready = sem("squares_of_last_tiles_added")
        hraw_ready = sem("h_ready")
        hh_ready = sem("h_hi_ready")
        hl_ready = sem("h_lo_ready")
        act_link = sem("act_link")
        dve_link = sem("dve_link")
        relu_used = sem("relu_used")
        gmv_ready = sem("gmlp_v_ready")
        var_ready = sem("var_ready")
        std_ready = sem("std_ready")
        wsT_ready = sem("wsT_ready")
        hsq_ready = sem("head_squares_ready")
        rs_ready = sem("inverse_rms_ready")
        r_ready = sem("residual_tile_ready")
        lg_ready = sem("logits_ready")
        p_ready = sem("probs_ready")
        pn_ready = sem("probs_normed")
        gla_dve = sem("gla_factors_ready")
        gla_act = sem("exp_done")
        exp_arg = sem("exp_argument_ready")
        negF_ready = sem("forget_sums_ready")
        inner_done = sem("gla_inner_done")
        y_src = sem("y_ready")
        yh_ready = sem("y_hi_ready")
        yl_ready = sem("y_lo_ready")
        merged_ready = sem("merged_ready")
        moe_act = sem("swiglu_act_ready")
        router_done = sem("router_weights_ready")
        ex_ready = sem("router_exp_argument")
        ex_done = sem("router_exp_done")
        gmlp_done = sem("gmlp_done")
        r_done = sem("residual_done")
        o_ready = sem("out_ready")

        def wk(name):
            return a[name][0].rearrange("(k p) n -> p k n", p=P)

        P1 = [("fm", D_IQ), ("tm", A_V), ("tm", A_V + 256), ("fm", A_U), ("fm", A_U + 256),
              ("tm", G_V), ("tm", G_V + 256), ("fm", G_Q), ("fm", G_K), ("fm", G_R), ("fm", G_R + 256),
              ("fm", D_Q), ("fm", D_Q + 256), ("fm", D_K), ("fm", D_K + 256), ("tm", D_V), ("tm", D_V + 256)]
        MOD1 = 8
        MODN = 24
        MOD_TILE = 13
        MOD_PE = (1, 3, 5)
        MODS_AT = [2] + [1] * 14 + [0] * 2
        SMALL_TILE = 24
        n_p1, n_m1, n_wo, n_moe = len(P1), 18, 4, 3 * N_EXP
        n_ff, n_p2, n_m2 = 3 * FF_UNITS, 12, 12
        P2 = [("fm", CC2), ("fm", CC2 + 256), ("fm", CI2), ("fm", CI2 + 256), ("fm", CB2), ("fm", CB2 + 256),
              ("fm", K2), ("fm", K2 + 256), ("fm", Q2), ("fm", Q2 + 256), ("tm", V2), ("tm", V2 + 256)]
        FORGET_AT, SPREAD_AT = 2, 4
        NCHUNK = n_p1 + n_m1 + n_wo + n_moe + n_ff + n_p2 + n_m2 + n_wo + n_ff

        block = ctx.enter_context(nc.Block())

        def mod_dve(n):
            return n - sum(m < n for m in MOD_PE)

        def mod_slot(n):
            if n < MOD1:
                x = (n + 2) % 4
                return (mod_more[:, x - 2] if x >= 2 else mod_raw[:, x]), mod_in[x], 16 * (n // 4 + 1)
            return mod_raw[:, n % 2], mod_in[n % 2], 16 * (n // 2 - 1)

        @block.sync
        def _(sp):
            count = [0, 0]

            def load(src, shape_k, n, more=0):
                c = count[0]
                if c >= RING:
                    sp.wait_ge(split, c - RING + 1 + more)
                dst = w_raw[:, c % RING, :].rearrange("p (k n) -> p k n", k=shape_k)
                sp.dma_start(dst, src).then_inc(w_in_sem[c % RING], 16)
                count[0] += 1

            def cols(name, c0):
                load(wk(name)[:, :, c0:c0 + 256], KT, 256)

            def load_mod(n):
                if 4 <= n < MOD1 and n - 4 not in MOD_PE:
                    sp.wait_ge(mod_used, mod_dve(n - 4) + 1)
                elif 4 <= n < MOD1:
                    g = MOD_TILE + n - 4
                    sp.wait_ge(ready[g % SLOTS], g // SLOTS + 1)
                elif n >= MOD1 + 2:
                    sp.wait_ge(mod_used, mod_dve(n - 2) + 1)
                dst, landed, _ = mod_slot(n)
                sp.dma_start(dst, wk("w_mod")[:, :, 256 * n:256 * n + 256]).then_inc(landed, 16)

            def row(name, r, n, tile, src=None):
                s = src if src is not None else a[name].rearrange("a (r n) -> (a r) n", n=P)
                sp.dma_start(tile[r:r + n, :], s).then_inc(vec_in, 16)

            sp.dma_start(x_tok[:, :, :], a["x"][0].rearrange("(t p) d -> p t d", p=P)).then_inc(x_in, 16)
            row("b_mod", 0, 48, vec_a)
            row("c", 48, 8, vec_a)
            row("g_norm1", 56, 8, vec_a)
            row("g_norm2", 64, 8, vec_a)
            row("b_branch_gate", 72, 24, vec_a, a["b_branch_gate"].rearrange("a b (r n) -> (a b r) n", n=P))
            row("gla_b_gate", 96, 2, vec_a)
            row("gla_norm_g", 98, 1, vec_a)
            row("dsa_qnorm_g", 99, 1, vec_a)
            row("dsa_knorm_g", 100, 1, vec_a)
            for n, name in enumerate(V2_NAMES):
                row(name, 8 * n, 8, vec_b)
            row("conv_w_2", CONV_ROW, 12, vec_b, a["conv_w_2"].rearrange("a j (r n) -> (a j r) n", n=P))
            load_mod(0)
            load_mod(1)
            sp.dma_start(oh_sb[0:32, :], one_hot).then_inc(oh_in, 16)
            sp.dma_start(relb[0:32, :], a["rel_bias"]).then_inc(oh_in, 16)
            sp.dma_start(meta_sb[0:META, :], a["meta_tokens_2"]).then_inc(oh_in, 16)
            w1 = wk("w_in")
            sp.dma_start(w_small[:, :, 0:16], w1[:, :, G_A:G_A + 16]).then_inc(small_in, 16)
            sp.dma_start(w_small[:, :, 16:80], w1[:, :, D_IK:D_IK + 64]).then_inc(small_in, 16)
            sp.dma_start(w_small[:, :, 80:144], w1[:, :, D_IK:D_IK + 64]).then_inc(small_in, 16)
            sp.dma_start(w_small[:, :, 144:148], w1[:, :, D_IW:D_IW + 4]).then_inc(small_in, 16)
            sp.dma_start(w_gate2[0:16, :], a["gla_w_gate2"][0]).then_inc(small_in, 16)
            sp.dma_start(w_route[:, :, 0:4], wk("w_group")).then_inc(small_in, 16)
            sp.dma_start(w_route[:, :, 4:20], wk("w_router")).then_inc(small_in, 16)
            sp.dma_start(b_route[:, 0:4], a["b_group"][0:1, :].to_broadcast([P, 4])).then_inc(small_in, 16)
            sp.dma_start(b_route[:, 4:20], a["b_router"][0:1, :].to_broadcast([P, 16])).then_inc(small_in, 16)
            sp.dma_start(w_forget[:, :, :], wk("w_in_2")[:, :, F2:F2 + 8]).then_inc(small_in, 16)
            sp.dma_start(b_fox[0:8, 0:1], a["b_forget_2"].rearrange("a h -> h a")).then_inc(small_in, 16)

            for s in range(SLOTS):
                sp.wait_ge(ready[s], 2)
            for n in range(2, MOD1):
                load_mod(n)
            for c in range(RING):
                cols("w_in", P1[c][1])
            sp.wait_ge(dist_ready, 1)
            sp.dma_start(dist_dram, dist_sb[0:4, :]).then_inc(dist_out, 16)
            sp.wait_ge(ready[SMALL_TILE % SLOTS], SMALL_TILE // SLOTS + 1)
            sp.wait_ge(hl_ready, KT)
            m = MOD1
            for n, k in enumerate(MODS_AT):
                for _ in range(k):
                    load_mod(m)
                    m += 1
                if RING + n < n_p1:
                    cols("w_in", P1[RING + n][1])
            sp.wait_ge(mod_used, mod_dve(MODN))
            sp.dma_start(ws[:, :, :], a["gmlp_w_s"][0].rearrange("g t s -> t g s")).then_inc(gm_in, 16)
            sp.dma_start(ln_rows[:, 0, :], a["gmlp_ln_g"][0:1, :].to_broadcast([P, DB])).then_inc(gm_in, 16)
            sp.dma_start(ln_rows[:, 1, :], a["gmlp_ln_b"][0:1, :].to_broadcast([P, DB])).then_inc(gm_in, 16)
            sp.dma_start(bs_rows[:, :, :], a["gmlp_b_s"].rearrange("a g t -> a (g t)").to_broadcast([P, 4 * P])
                         .rearrange("p (g t) -> p g t", g=4)).then_inc(gm_in, 16)

            def merge_loads(w_gate, gate0, w_up, n_br):
                for mq in range(2):
                    c0 = count[0]
                    with sp.Fori(0, n_br) as n:
                        count[0] = c0
                        for j in range(2):
                            base = gate0 + 512 * mq + 256 * j
                            load(wk(w_gate)[:, :, bass.ds(n * D + base, 256)], KT, 256, n * 3)
                        load(w_up(n, mq), BT, 512, n * 3)
                    count[0] = c0 + 3 * n_br

            merge_loads("w_in", GATES, lambda n, mq: a["w_branch"][0].rearrange("b (k p) n -> p b k n", p=P)[
                :, bass.ds(n, 1), :, 512 * mq:512 * mq + 512].rearrange("p b k n -> p (b k) n"), 3)
            for j in range(4):
                cols("w_out", 256 * j)

            def swiglu_loads(gate, up, down, units):
                load(gate(0), KT, 256)
                load(up(0), KT, 256)
                c0 = count[0]
                with sp.Fori(0, units - 1) as i:
                    count[0] = c0
                    load(gate(i + 1), KT, 256, i * 3)
                    load(up(i + 1), KT, 256, i * 3)
                    load(down(i), 2, D, i * 3)
                count[0] = c0 + 3 * (units - 1)
                load(down(units - 1), 2, D)

            swiglu_loads(lambda e: a["w_exp_gate"][0].rearrange("e (k p) f -> p e k f", p=P)[:, bass.ds(e, 1)].rearrange("p e k f -> p (e k) f"),
                         lambda e: a["w_exp_up"][0].rearrange("e (k p) f -> p e k f", p=P)[:, bass.ds(e, 1)].rearrange("p e k f -> p (e k) f"),
                         lambda e: a["w_exp_down"][0].rearrange("e (k p) f -> p e k f", p=P)[:, bass.ds(e, 1)].rearrange("p e k f -> p (e k) f"),
                         N_EXP)

            def ffn_loads(w_i, w_o):
                swiglu_loads(lambda e: wk(w_i)[:, :, bass.ds(e * 256, 256)],
                             lambda e: wk(w_i)[:, :, bass.ds(e * 256 + D_FF, 256)],
                             lambda e: wk(w_o)[:, bass.ds(e * 2, 2), :], FF_UNITS)

            ffn_loads("w_ffn1_in_2", "w_ffn1_out_2")
            for _, c0 in P2:
                cols("w_in_2", c0)
            for mq in range(2):
                for n in range(2):
                    for j in range(2):
                        cols("w_in_2", GA2 + D * n + 512 * mq + 256 * j)
                    load(wk(("w_attn_branch_2", "w_conv_branch_2")[n])[:, :, 512 * mq:512 * mq + 512], BT, 512)
            for j in range(4):
                cols("w_out_2", 256 * j)
            ffn_loads("w_ffn2_in_2", "w_ffn2_out_2")
            assert count[0] == NCHUNK
            for t in range(NTOK):
                sp.wait_ge(o_ready, 2 * (t + 1))
                sp.dma_start(out[0, P * t:P * t + P, :], o_tok[:, t, :]).then_inc(out_done, 16)
            sp.wait_ge(out_done, 16 * NTOK)

        @block.gpsimd
        def _(pool):
            pool.memset(ident[:, :], 0.0).then_inc(consts, 1)
            pool.memset(ones[:, :], 1.0).then_inc(consts, 1)
            pool.memset(outside[:, :], 0.0).then_inc(consts, 1)
            pool.memset(eps[:, 0:1], EPS).then_inc(consts, 1)
            pool.memset(eps[:, 1:2], 1.0).then_inc(consts, 1)
            pool.wait_ge(consts, 5)
            pool.affine_select(out=ident[:, :], in_=ident[:, :], compare_op=ALU.not_equal, fill=1.0, base=0,
                               pattern=[[-1, P]], channel_multiplier=1).then_inc(consts, 1)
            pool.affine_select(out=tri[:, :], in_=ones[:, :], compare_op=ALU.is_ge, fill=0.0, base=0,
                               pattern=[[1, P]], channel_multiplier=-1).then_inc(consts, 1)
            pool.affine_select(out=outside[:, :], in_=outside[:, :], compare_op=ALU.is_ge, fill=OUTSIDE, base=0,
                               pattern=[[-1, P]], channel_multiplier=1).then_inc(consts, 1)

            def split_chunk(c, s, more=0):
                pool.wait_ge(hi_done, c + 1 + more * RING)
                pool.tensor_tensor(w_lo[:, s, :], w_raw[:, s, :], w_hi[:, s, :].bitcast(F32), ALU.subtract).then_inc(split, 1)

            for c in range(RING):
                split_chunk(c, c)
            rounds = (NCHUNK - RING) // RING
            with pool.Fori(0, rounds) as i:
                for s in range(RING):
                    split_chunk(RING + s, s, i)
            for c in range(RING * (rounds + 1), NCHUNK):
                split_chunk(c, c % RING)

        @block.tensor
        def _(pe):
            W = PsumWalk(pe, ready, free)
            mm = nc.tensor.matmul
            cur = {"c": 0, "more": 0}

            def begin_chunk():
                c = cur["c"]
                pe.wait_ge(split, c + 1 + cur["more"])
                cur["c"] += 1
                cur["fresh"] = True
                return c % RING

            def product(o, l, r, **k):
                ins = mm(o, l, r, **k)
                if cur["fresh"]:
                    ins.then_inc(begun, 1)
                    cur["fresh"] = False
                return ins

            def three(outs, lhs, rhs, first, last):
                for n, (l, r) in enumerate(((0, 0), (0, 1), (1, 0))):
                    for o, cs in outs:
                        ins = product(o, lhs[l], rhs[r][:, cs], start=first and n == 0, stop=last and n == 2)
                return ins

            def outs_of(s, T):
                return [(PS[:, s, b, 0:n], slice(c0, c0 + n)) for b, (c0, n) in enumerate(halves(T))]

            def fm_chunk(nk, mt, rh, rl_, T):
                s_w = begin_chunk()
                hi = w_hi[:, s_w, :].rearrange("p (k n) -> p k n", k=nk)
                lo = w_lo[:, s_w, :].rearrange("p (k n) -> p k n", k=nk)
                for m in range(mt):
                    s = W.claim()
                    for k in range(nk):
                        cs = slice(P * m, P * m + P)
                        if cur["h"] is not None and m == 0:
                            pe.wait_ge(hl_ready, cur["h"] + k + 1)
                        ins = three(outs_of(s, T), (hi[:, k, cs], lo[:, k, cs]), (rh(k), rl_(k)), k == 0, k == nk - 1)
                    W.made(ins)
                cur["h"] = None

            def h_operands(t0_, T):
                return (lambda k: HH[:, k, t0_:t0_ + T]), (lambda k: HL[:, k, t0_:t0_ + T])

            def tm_chunk(tiles):
                s_w = begin_chunk()
                hi = w_hi[:, s_w, :].rearrange("p (k n) -> p k n", k=KT)
                lo = w_lo[:, s_w, :].rearrange("p (k n) -> p k n", k=KT)
                for t_0, tn in tiles:
                    s = W.claim()
                    for k in range(KT):
                        for n, (l, r) in enumerate(((HH, hi), (HH, lo), (HL, hi))):
                            ins = product(PS[0:tn, s, 0, 0:256], l[:, k, t_0:t_0 + tn], r[:, k, :],
                                          start=k == 0 and n == 0, stop=k == KT - 1 and n == 2)
                    W.made(ins)

            hcount = {"sq": 0, "sum": 0, "hl": 0, "hsq": 0, "mod": 0, "rs": 0}
            cur["h"] = None

            def spread_rms(c0, T):
                G, J = token_groups(T)
                s = W.claim()
                for j in range(J):
                    bank, col = (0, G * j) if T <= 512 else (j // 3, G * (j % 3))
                    ins = mm(PS[:, s, bank, col:col + G], rsc[0:G, c0 + j:c0 + j + 1].to_broadcast([G, P]), ident[0:G, 0:G],
                             start=True, stop=True)
                W.made(ins)

            def sum_squares(T, sq, last=KT - 1):
                G, J = token_groups(T)
                s = W.claim()
                for k in range(last + 1):
                    if k == last and last < KT - 1:
                        hcount["sum"] += 1
                        pe.wait_ge(sqsum_ready, hcount["sum"])
                    else:
                        pe.wait_ge(sq_ready, hcount["sq"] + k + 1)
                    for j in range(J):
                        ins = mm(PS[0:G, s, 0, j:j + 1], sq[:, k, G * j:G * j + G], ones[:, 0:1],
                                 start=k == 0 and j == 0, stop=k == last, skip_group_check=True)
                hcount["sq"] += KT
                W.made(ins)

            def spread_root(T):
                hcount["rs"] += 1
                pe.wait_ge(rs_ready, hcount["rs"])
                spread_rms(0, T)

            def norm(T):
                sum_squares(T, Hf, SQ_OWN)
                spread_root(T)

            def await_h(now=True):
                if now:
                    pe.wait_ge(hl_ready, hcount["hl"] + KT)
                else:
                    cur["h"] = hcount["hl"]
                hcount["hl"] += KT

            def mod_tile():
                n = hcount["mod"]
                hcount["mod"] += 1
                if n in MOD_PE:
                    raw, landed, count = mod_slot(n)
                    pe.wait_ge(landed, count)
                    s = W.claim()
                    for m in range(2):
                        for k in range(KT):
                            ins = mm(PS[:, s, 0, m:m + 1], raw[:, k, P * m:P * m + P], c_act[:, k:k + 1],
                                     start=k == 0, stop=k == KT - 1)
                else:
                    d = mod_dve(n)
                    pe.wait_ge(macc_ready, d + 1)
                    s = W.claim()
                    for m in range(2):
                        ins = mm(PS[:, s, 0, m:m + 1], macc[:, d % 2, P * m:P * m + P], ones[:, 0:1], start=True, stop=True)
                W.made(ins)

            pe.wait_ge(consts, 8)
            pe.wait_ge(x_in, 16)
            for k in range(KT):
                s = W.claim()
                for t in range(NTOK):
                    ins = nc.tensor.transpose(PS[:, s, 0, P * t:P * t + P], x_tok[:, t, P * k:P * k + P], ident[:, :])
                W.made(ins)
            pe.wait_ge(vec_in, 16 * 16)
            for rows, src in ((V1_ROWS, vec_a), (V2_ROWS, vec_b)):
                s = W.claim()
                W.made(nc.tensor.transpose(PS[:, s, 0, 0:rows], src[0:rows, :], ident[0:rows, 0:rows]))
            pe.wait_ge(oh_in, 48)
            s = W.claim()
            for k in range(KT):
                ins = nc.tensor.transpose(PS[:, s, 0, META * k:META * k + META], meta_sb[0:META, P * k:P * k + P],
                                          ident[0:META, 0:META])
            W.made(ins)
            s = W.claim()
            mm(PS[0:4, s, 0, 0:512], relb[0:32, :], oh_sb[0:32, 0:512], start=True, stop=True)
            W.made(mm(PS[0:4, s, 1, 0:128], relb[0:32, :], oh_sb[0:32, 512:640], start=True, stop=True))
            sum_squares(SEQ, squares1, SQ_OWN)
            pe.wait_ge(cact_ready, 1)
            assert W.g == MOD_TILE
            for n in range(MOD1):
                mod_tile()
            spread_root(SEQ)
            pe.wait_ge(small_in, 16 * 11)
            g0, slots = W.g, []
            for x in range(3):
                slots.append(W.claim())
                W.g += 1
            W.g = g0
            for k in range(KT):
                pe.wait_ge(hh_ready, k + 1)
                for s, c0, n in ((slots[0], 0, 16), (slots[1], 16, 128)):
                    ins = mm(PS[0:n, s, 0, :], w_small[:, k, c0:c0 + n], Hf[:, k, 0:SEQ], start=k == 0, stop=k == KT - 1)
                    if k == KT - 1:
                        W.made(ins)
                for t in range(NTOK):
                    ins = mm(PS[:, slots[2], 0, 4 * t:4 * t + 4], Hf[:, k, P * t:P * t + P], w_small[:, k, 144:148],
                             start=k == 0 and t == 0, stop=k == KT - 1, skip_group_check=True)
            W.made(ins)
            await_h(now=False)
            rh, rlo = h_operands(0, SEQ)
            tok_tiles = [(P * t, P) for t in range(NTOK)]
            for n, (kind, _) in enumerate(P1):
                if n == n_p1 - 1:
                    pe.wait_ge(gm_in, 64)
                    s = W.claim()
                    for g in range(4):
                        ins = nc.tensor.transpose(PS[:, s, 0, P * g:P * g + P], ws[:, g, :], ident[:, :])
                    W.made(ins)
                if kind == "fm":
                    fm_chunk(KT, 2, rh, rlo, SEQ)
                else:
                    tm_chunk(tok_tiles)
                if n == 0:
                    W.wait_released(W.g - 1)
                    W.wait_released(W.g - 2)
                    for i in range(1, NTOK):
                        for h in range(4):
                            s = W.claim()
                            b = 64 * (h % 2)
                            W.made(mm(PS[:, s, 0, 0:(i + 1) * P], iq[b:b + 64, h // 2, P * i:P * i + P],
                                      ik[b:b + 64, 0:(i + 1) * P], start=True, stop=True))
                for _ in range(MODS_AT[n]):
                    mod_tile()

            pe.wait_ge(wsT_ready, 1)
            pe.wait_ge(gmv_ready, 1)
            for g in range(4):
                s = W.claim()
                for t in range(NTOK):
                    ins = mm(PS[:, s, 0, P * t:P * t + P], v[:, t, P * g:P * g + P], wsT[:, g, :], start=True, stop=True)
                W.made(ins)

            def head_norms(n):
                s = W.claim()
                for x in range(n):
                    hcount["hsq"] += 1
                    pe.wait_ge(hsq_ready, hcount["hsq"])
                    for t in range(NTOK):
                        ins = mm(PS[:, s, 0, NTOK * x + t:NTOK * x + t + 1], sqh[:, x, P * t:P * t + P], ones[:, 0:1],
                                 start=x == 0 and t == 0, stop=True, skip_group_check=True)
                W.made(ins)
                hcount["rs"] += 1
                pe.wait_ge(rs_ready, hcount["rs"])
                for x in range(n):
                    spread_rms(NTOK * x, SEQ)

            att = {"n": 0}

            def attention(combos, logits, keys, pr, pT, values, o):
                N = len(combos)
                for n in range(N + 3):
                    if n < N:
                        s = W.claim()
                        W.made(logits(s, *combos[n]))
                    if 0 <= n - 2 < N:
                        i, h = combos[n - 2]
                        att["n"] += 1
                        pe.wait_ge(pn_ready, att["n"])
                        s = W.claim()
                        for c0, kt, kn in keys(i):
                            bank, col = (0, P * kt) if kt < 4 else (1, 0)
                            ins = nc.tensor.transpose(PS[0:kn, s, bank, col:col + P], pr[:, (n - 2) % 3, c0:c0 + kn], ident[:, :])
                        att[n - 2] = W.g
                        W.made(ins)
                    if 0 <= n - 3 < N:
                        i, h = combos[n - 3]
                        W.wait_released(att[n - 3])
                        s = W.claim()
                        ks = keys(i)
                        for x, (c0, kt, kn) in enumerate(ks):
                            ins = mm(o(s, h), values(kt, kn, h), pT[0:kn, (n - 3) % 2, kt, :], start=x == 0, stop=x == len(ks) - 1)
                        W.made(ins)

            head_norms(8)
            for b in range(1, 5):
                W.wait_released(W.g - b)
            combos1 = [(i, h) for i in range(NTOK) for h in range(4)]
            attention(combos1,
                      lambda s, i, h: mm(PS[:, s, 0, 0:(i + 1) * P], dq[:, h, P * i:P * i + P], dk[:, h, 0:(i + 1) * P],
                                         start=True, stop=True),
                      lambda i: [(P * j, j, P) for j in range(i + 1)], pr1, pT1,
                      lambda kt, kn, h: dv[:, kt, P * h:P * h + P], lambda s, h: PS[:, s, 0, 0:P])

            for j in range(2):
                s = W.claim()
                W.made(mm(PS[:, s, 0, :], w_gate2[0:16, P * j:P * j + P], ga[0:16, 0:SEQ], start=True, stop=True))
            for j in range(2):
                pe.wait_ge(gla_dve, j + 1)
                for hh in range(2):
                    s = W.claim()
                    hp = slice(64 * hh, 64 * hh + 64)
                    for c in range(8):
                        op = slice(64 * (c % 2), 64 * (c % 2) + 64)
                        for q in range(4):
                            ins = mm(PS[op, s, 0, CHUNK * (c // 2):CHUNK * (c // 2) + CHUNK], Kp[hp, q, CHUNK * c:CHUNK * c + CHUNK],
                                     Qp[hp, q, CHUNK * c:CHUNK * c + CHUNK], start=q == 0, stop=q == 3)
                    W.made(ins)
                s = W.claim()
                for t in range(NTOK):
                    ins = nc.tensor.transpose(PS[:, s, 0, P * t:P * t + P], kk[:, j, P * t:P * t + P], ident[:, :])
                W.made(ins)
            W.wait_released(W.g - 1)
            W.wait_released(W.g - 4)
            for c in range(7):
                s = W.claim()
                cp = slice(64 * (c % 2), 64 * (c % 2) + 64)
                for j in range(2):
                    for hh in range(2):
                        h = 2 * j + hh
                        ins = mm(PS[64 * hh:64 * hh + 64, s, 0, P * j:P * j + P], kkT[cp, j, c // 2, 64 * hh:64 * hh + 64],
                                 gv[cp, c // 2, P * h:P * h + P], start=True, stop=True)
                W.made(ins)
            pe.wait_ge(gla_dve, 3)
            for h in range(4):
                s = W.claim()
                j, hp = h // 2, slice(64 * (h % 2), 64 * (h % 2) + 64)
                for c in (0, 2, 4, 6, 1, 3, 5, 7):
                    cp = slice(64 * (c % 2), 64 * (c % 2) + 64)
                    ins = mm(PS[:, s, c % 2, CHUNK * (c // 2):CHUNK * (c // 2) + CHUNK], gv[cp, c // 2, P * h:P * h + P],
                             attT[cp, h, c // 2, :], start=c < 2, stop=False, skip_group_check=True)
                ins.then_inc(inner_done, 1)
                pe.wait_ge(inner_done, h + 1)
                for c in range(1, 8):
                    ins = mm(PS[:, s, c % 2, CHUNK * (c // 2):CHUNK * (c // 2) + CHUNK], Sall[hp, c, j, :],
                             qe[hp, j, CHUNK * c:CHUNK * c + CHUNK], start=False, stop=True, skip_group_check=True)
                W.made(ins)
            head_norms(4)

            ycount = {"yl": 0}

            def merge(n_br, yh, yl, t0_):
                rh_, rl_ = h_operands(t0_, SEQ)
                for mq in range(2):
                    c0, g0 = cur["c"], W.g

                    def body(n, n_static):
                        for _ in range(2):
                            fm_chunk(KT, 2, rh_, rl_, SEQ)
                        if n_static is not None:
                            if mq == 0 and n_static == 0:
                                ycount["yl"] += BT * n_br
                                pe.wait_ge(yl_ready, ycount["yl"])
                        fm_chunk(BT, 4, lambda k: yk(yh, n, k), lambda k: yk(yl, n, k), SEQ)

                    def yk(y, n, k):
                        if isinstance(n, int):
                            return y[:, BT * n + k, :]
                        return y[:, bass.ds(n * BT + k, 1), :].rearrange("p a n -> p (a n)")

                    body(0, 0)
                    with pe.Fori(0, n_br - 1) as i:
                        cur["c"], W.g = c0 + 3, g0 + 8
                        cur["more"], W.more = i * 3, i * 2
                        body(i + 1, None)
                    cur["c"], W.g = c0 + 3 * n_br, g0 + 8 * n_br
                    cur["more"], W.more = 0, 0

            merge(3, YH, YL, 0)

            def out_projection():
                await_h(now=False)
                rh_, rl_ = h_operands(0, SEQ)
                for _ in range(4):
                    fm_chunk(KT, 2, rh_, rl_, SEQ)

            out_projection()

            norm(SEQ)
            s = W.claim()
            for k in range(KT):
                pe.wait_ge(hh_ready, 2 * KT + k + 1)
                for t in range(NTOK):
                    ins = mm(PS[:, s, 0, 20 * t:20 * t + 20], Hf[:, k, P * t:P * t + P], w_route[:, k, :],
                             start=k == 0 and t == 0, stop=k == KT - 1, skip_group_check=True)
            W.made(ins)
            await_h(now=False)

            def spread_routing():
                pe.wait_ge(router_done, 1)
                s = W.claim()
                for t in range(NTOK):
                    ins = nc.tensor.transpose(PS[0:16, s, 0, P * t:P * t + P], rc[:, t, :], ident[:, :])
                W.made(ins)
                W.wait_released(W.g - 1)
                for e in range(N_EXP):
                    s = W.claim()
                    W.made(mm(PS[:, s, 0, :], ident[0:16, e:e + 1].to_broadcast([16, P]), combT[0:16, :], start=True, stop=True))

            units_done = {"n": 0}

            def swiglu(units, T, t0_, between=None):
                rh_, rl_ = h_operands(t0_, T)
                base = units_done["n"]

                def up(between=None):
                    fm_chunk(KT, 2, rh_, rl_, T)
                    if between is not None:
                        between()
                    fm_chunk(KT, 2, rh_, rl_, T)

                def down(n, par, more=0):
                    pe.wait_ge(moe_act, base + n + 1 + more)
                    fm_chunk(2, KT, lambda k: ah[:, par, k, 0:T], lambda k: al[:, par, k, 0:T], T)

                up(between)
                c0, g0 = cur["c"], W.g
                pairs = (units - 1) // 2
                with pe.Fori(0, pairs) as i:
                    cur["c"], W.g = c0, g0
                    cur["more"], W.more = i * 6, i * 6
                    for par in range(2):
                        up()
                        down(par, par, i * 2)
                cur["c"], W.g = c0 + 6 * pairs, g0 + 24 * pairs
                cur["more"], W.more = 0, 0
                for n in range(2 * pairs, units):
                    if n + 1 < units:
                        up()
                    down(n, n % 2)
                units_done["n"] += units

            swiglu(N_EXP, SEQ, 0, spread_routing)

            norm(TALL)
            await_h(now=False)
            swiglu(FF_UNITS, TALL, 0)
            norm(TALL)
            norm(TALL)
            await_h(now=False)
            tok5 = [(META + P * t, P) for t in range(NTOK)] + [(0, META)]
            full, real = h_operands(0, TALL), h_operands(META, SEQ)
            for n_p, (kind, c0) in enumerate(P2):
                if n_p == FORGET_AT:
                    s = W.claim()
                    for k in range(KT):
                        for b, (x0, n) in enumerate(halves(TALL)):
                            ins = mm(PS[0:8, s, b, 0:n], w_forget[:, k, :], Hf[:, k, x0:x0 + n], start=k == 0, stop=k == KT - 1)
                    W.made(ins)
                if n_p == SPREAD_AT:
                    pe.wait_ge(negF_ready, 1)
                    for h in range(8):
                        s = W.claim()
                        for b, (x0, n) in enumerate(halves(TALL)):
                            ins = mm(PS[:, s, b, 0:n], ident[0:8, h:h + 1].to_broadcast([8, P]), negF[0:8, x0:x0 + n],
                                     start=True, stop=True)
                        W.made(ins)
                if kind == "tm":
                    tm_chunk(tok5)
                elif c0 in (CB2, CB2 + 256, Q2, Q2 + 256):
                    fm_chunk(KT, 2, *real, SEQ)
                else:
                    fm_chunk(KT, 2, *full, TALL)

            def fox_logits(s, i, h):
                b = 64 * (h % 2)
                n_all = META + P * (i + 1)
                for bank, c0, n in ((0, 0, min(512, n_all)), (1, 512, n_all - 512)):
                    if n > 0:
                        ins = mm(PS[:, s, bank, 0:n], q2[b:b + 64, h // 2, P * i:P * i + P], k2[b:b + 64, h // 2, c0:c0 + n],
                                 start=True, stop=True)
                return ins

            combos2 = [(i, h) for i in range(NTOK) for h in range(8)]
            W.wait_released(W.g - 1)
            W.wait_released(W.g - 2)
            W.wait_released(W.g - 3)
            W.wait_released(W.g - 4)
            attention(combos2, fox_logits, lambda i: [(0, 4, META)] + [(META + P * j, j, P) for j in range(i + 1)],
                      pr2, pT2, lambda kt, kn, h: v2[0:kn, kt, 64 * h:64 * h + 64],
                      lambda s, h: PS[64 * (h % 2):64 * (h % 2) + 64, s, 0, 0:P])
            merge(2, YH2, YL2, META)
            out_projection()
            norm(SEQ)
            norm(SEQ)
            await_h(now=False)
            swiglu(FF_UNITS, SEQ, 0)
            norm(SEQ)
            pe.wait_ge(r_done, 1)
            for t in range(NTOK):
                for half in range(2):
                    s = W.claim()
                    for k in range(4):
                        ins = nc.tensor.transpose(PS[:, s, 0, P * k:P * k + P],
                                                  R[:, 4 * half + k, META + P * t:META + P * t + P], ident[:, :])
                    W.made(ins)
            assert cur["c"] == NCHUNK

        @block.scalar
        def _(act):
            W = PsumWalk(act, ready, free)
            L = Link(act, act_link)
            af = nc.scalar.activation
            n_ = {"r": 0, "hraw": 0, "hh": 0, "hn": 0, "lg": 0, "ysrc": 0, "merged": 0, "std": 0}

            def ps(s, T=SEQ):
                return PS[:, s, 0, 0:T] if T <= 512 else PS[:, s, 0:2, 0:T // 2]

            def sv(ap, T):
                return ap if T <= 512 else ap.rearrange("p (b n) -> p b n", b=2)

            def evac(out_, func=ACT.Copy, src=None, **k):
                s = W.arrive()
                W.release(af(out_, ps(s) if src is None else src(s), func, **k))

            def root(T):
                G, J = token_groups(T)
                s = W.arrive()
                W.release(af(rsc[0:G, 0:J], PS[0:G, s, 0, 0:J], ACT.Sqrt, scale=1.0 / D, bias=eps[0:G, 0:1]))

            def norm(T, src, shift=None, split=True, tiles=True):
                for k in range(KT):
                    if tiles:
                        W.wait_released(W.g - KT + k)
                    else:
                        n_["r"] += 1
                        act.wait_ge(r_ready, n_["r"])
                    af(Hf[:, k, 0:T], src(k), ACT.Square).then_inc(sq_ready, 1)
                root(T)
                W.skip(1)
                if split:
                    shift_and_split(T, shift)

            def shift_and_split(T, shift=None):
                for k in range(KT):
                    if k < KT - 1:
                        n_["hraw"] += 1
                        act.wait_ge(hraw_ready, n_["hraw"])
                    else:
                        W.wait_released(W.g - 1)
                    if shift is not None:
                        L(af(Hf[:, k, 0:T], Hf[:, k, 0:T], ACT.Identity, bias=shift(k)))
                    af(HH[:, k, 0:T], Hf[:, k, 0:T], ACT.Copy).then_inc(hh_ready, 1)

            hi = {"c": 0, "rounds": 0}

            def next_hi():
                c = hi["c"]
                if c >= NCHUNK:
                    return
                rounds = hi["rounds"]
                act.wait_ge(w_in_sem[c % RING], 16 * (c // RING + 1) + rounds * 16)
                if c >= RING:
                    act.wait_ge(begun, c - 1 + rounds * RING)
                af(w_hi[:, c % RING, :], w_raw[:, c % RING, :], ACT.Copy).then_inc(hi_done, 1)
                hi["c"] += 1

            for k in range(KT):
                s = W.arrive()
                ins = af(R[:, k, META:TALL], ps(s), ACT.Copy)
                W.release(ins)
            W.skip(2)
            s = W.arrive()
            W.release(af(R[:, :, 0:META], PS[:, s, 0, 0:KT * META].rearrange("p (k t) -> p k t", t=META), ACT.Copy))
            W.skip(1)
            act.wait_ge(cols_ready, 1)
            af(c_act[:, :], C1[:, V1["c"]:V1["c"] + KT], ACT.Silu).then_inc(cact_ready, 1)
            real = lambda k: R[:, k, META:TALL]
            every = lambda k: R[:, k, 0:TALL]
            y_real = lambda k: yacc[:, k, 0:SEQ]
            W.wait_released(W.g - 2)
            for k in range(KT):
                af(squares1[:, k, :], real(k), ACT.Square).then_inc(sq_ready, 1)
            root(SEQ)
            W.skip(MOD1 + 1)
            shift_and_split(SEQ, lambda k: modc[:, k:k + 1])
            next_hi()
            next_hi()
            evac(ga[0:16, 0:SEQ], src=lambda s: PS[0:16, s, 0, :])
            evac(ik[:, :])
            evac(iw[:, :, :], src=lambda s: PS[:, s, 0, 0:16].rearrange("p (t h) -> p t h", h=4))

            def tm(dst, c0, func=ACT.Copy):
                for t in range(NTOK):
                    evac(dst[:, t, c0:c0 + 256], func, src=lambda s: PS[:, s, 0, 0:256])

            def fm(dst, m0, func=ACT.Copy):
                for m in range(2):
                    evac(dst[:, m0 + m, :], func)

            plan = {D_IQ: lambda: fm(iq, 0), A_V: lambda: tm(v, 0, ACT.Gelu_apprx_tanh),
                    A_V + 256: lambda: tm(v, 256, ACT.Gelu_apprx_tanh), A_U: lambda: fm(u, 0, ACT.Gelu_apprx_tanh),
                    A_U + 256: lambda: fm(u, 2, ACT.Gelu_apprx_tanh), G_V: lambda: tm(gv, 0), G_V + 256: lambda: tm(gv, 256),
                    G_Q: lambda: fm(gq, 0), G_K: lambda: fm(gk, 0), G_R: lambda: fm(gr, 0, ACT.Silu),
                    G_R + 256: lambda: fm(gr, 2, ACT.Silu), D_Q: lambda: fm(dq, 0), D_Q + 256: lambda: fm(dq, 2),
                    D_K: lambda: fm(dk, 0), D_K + 256: lambda: fm(dk, 2), D_V: lambda: tm(dv, 0), D_V + 256: lambda: tm(dv, 256)}
            for n, (_, c0) in enumerate(P1):
                if n == n_p1 - 1:
                    evac(wsT[:, :, :], src=lambda s: PS[:, s, 0, :].rearrange("p (g t) -> p g t", g=4))
                    act.wait_ge(var_ready, 1)
                    af(rstd[:, :], mv[:, :, 1], ACT.Sqrt, bias=eps[:, 0:1]).then_inc(std_ready, 1)
                next_hi()
                if n == 15:
                    act.wait_ge(relu_used, 12)
                plan[c0]()
                if n == 0:
                    for x in range(12):
                        if x >= 2:
                            act.wait_ge(relu_used, x - 1)
                        s = W.arrive()
                        w = (x // 4 + 2) * P
                        W.release(af(relu_s[:, x % 2, 0:w], PS[:, s, 0, 0:w], ACT.Relu))
                W.skip(MODS_AT[n])

            W.skip(4)

            def head_norms(count):
                s = W.arrive()
                W.release(af(rsc[:, 0:NTOK * count], PS[:, s, 0, 0:NTOK * count], ACT.Sqrt, scale=1.0 / P, bias=eps[:, 0:1]))
                W.skip(count)

            def attention(combos, width, lg, pr, scale, pT, keys, dst, o):
                N = len(combos)
                for n in range(N + 3):
                    if n < N:
                        i, h = combos[n]
                        W.skip(1)
                        n_["lg"] += 1
                        act.wait_ge(lg_ready, n_["lg"])
                        w, c = width(i), n % 32
                        af(pr[:, n % 3, 0:w], lg[:, n % 2, 0:w], ACT.Exp, bias=nmax[:, c:c + 1], scale=scale,
                           accum_out=den[:, c:c + 1]).then_inc(p_ready, 1)
                    if 0 <= n - 2 < N:
                        i, h = combos[n - 2]
                        s = W.arrive()
                        par = (n - 2) % 2
                        if keys:
                            L.mark(af(pT[0:META, par, 4, :], PS[0:META, s, 1, 0:P], ACT.Copy))
                        W.release(af(pT[:, par, 0:i + 1, :], PS[:, s, 0, 0:(i + 1) * P].rearrange("p (k t) -> p k t", t=P), ACT.Copy))
                    if 0 <= n - 3 < N:
                        i, h = combos[n - 3]
                        s = W.arrive()
                        W.release(af(dst(i, h), o(s, h), ACT.Copy))

            act.wait_ge(dist_out, 16)
            act.wait_ge(gmlp_done, 1)
            for h in range(4):
                act.dma_start(bias_rev[:, h, :], bass.AP(dist_dram.tensor, 640 * h, [[1, P], [1, SEQ]])).then_inc(bias_in, 16)
            head_norms(8)
            combos1 = [(i, h) for i in range(NTOK) for h in range(4)]
            attention(combos1, lambda i: (i + 1) * P, lg1, pr1, 1.0, pT1, False,
                      lambda i, h: dq[:, h, P * i:P * i + P], lambda s, h: PS[:, s, 0, 0:P])

            for j in range(2):
                s = W.arrive()
                W.release(af(Bc[:, j, :], ps(s), ACT.Identity, bias=C1[:, V1["gla_b_gate"] + j:V1["gla_b_gate"] + j + 1]))
            W.wait_released(W.g - 2)
            W.wait_released(W.g - 1)
            for j in range(2):
                L.mark(af((t0, t1)[j][:, :], Bc[:, j, :], ACT.Abs))
            L.wait()
            for j in range(2):
                L.mark(af((t0, t1)[j][:, :], (t0, t1)[j][:, :], ACT.Exp, scale=-1.0))
            L.wait()
            for j in range(2):
                af((t0, t1)[j][:, :], (t0, t1)[j][:, :], ACT.Ln, bias=eps[:, 1:2]).then_inc(gla_act, 1)
            seq = 0
            for j in range(2):
                for _ in range(7):
                    seq += 1
                    act.wait_ge(exp_arg, seq)
                    b = (t0, t1, t2)[(seq - 1) % 3]
                    if (seq - 1) % 7 >= 3:
                        q = (seq - 1) % 7 - 3
                        bb = b[:, :].rearrange("p (c t) -> p c t", c=8)[:, :, SUB * q:CHUNK]
                    else:
                        bb = b[:, :]
                    af(bb, bb, ACT.Exp, scale=1.0 / 16).then_inc(gla_act, 1)
                W.skip(2)
                s = W.arrive()
                W.release(af(kkT[:, j, :, :], PS[:, s, 0, :].rearrange("p (t d) -> p t d", t=NTOK), ACT.Copy))
            act.wait_ge(exp_arg, seq + 1)
            af(ebl[:, :, :], ebl[:, :, :], ACT.Exp, scale=1.0 / 16).then_inc(gla_act, 1)
            W.skip(7)
            for h in range(4):
                evac(og[:, h, :].rearrange("p (c b t) -> p b c t", b=2, t=CHUNK),
                     src=lambda s: PS[:, s, :, 0:SEQ // 2].rearrange("p b (c t) -> p b c t", t=CHUNK))
            head_norms(4)

            def merge(srcs, yh, sg_, n_br, bias):
                n_["ysrc"] += 1
                act.wait_ge(y_src, n_["ysrc"])
                for n, y in enumerate(srcs):
                    af(yh[:, n, :], y, ACT.Copy).then_inc(yh_ready, 1)
                for mq in range(2):
                    g0 = W.g

                    def body(n):
                        for m in range(4):
                            if m % 2 == 0:
                                next_hi()
                            if not (mq == 0 and isinstance(n, int)):
                                W.wait_released(g_base[0] - 4 + m)
                            k = {} if bias is None else {"bias": bias(n, 4 * mq + m)}
                            evac(sg_[:, m, :], ACT.Sigmoid, **k)
                        next_hi()
                        W.skip(4)

                    g_base = [g0]
                    c0 = hi["c"]
                    if mq == 0:
                        act.wait_ge(yl_ready, n_["yl"])
                    body(0)
                    with act.Fori(0, n_br - 1) as i:
                        W.g = g0 + 8
                        g_base[0] = g0 + 8
                        W.more = i * 2
                        hi["c"], hi["rounds"] = c0 + 3, i
                        body(i + 1)
                    W.more = 0
                    hi["c"], hi["rounds"] = c0 + 3 * n_br, 0
                    W.g = g0 + 8 * n_br

            def merged_split():
                n_["merged"] += 1
                act.wait_ge(merged_ready, n_["merged"])
                for k in range(KT):
                    af(HH[:, k, 0:SEQ], Hf[:, k, 0:SEQ], ACT.Copy).then_inc(hh_ready, 1)

            n_["yl"] = 12
            bcol = V1["b_branch_gate"]

            def gate_bias(n, m):
                if isinstance(n, int):
                    return C1[:, bcol + KT * n + m:bcol + KT * n + m + 1]
                return C1[:, bass.ds(n * KT + bcol + m, 1)]

            merge([u[:, k, :] for k in range(4)] + [gr[:, k, :] for k in range(4)] + [dq[:, k, :] for k in range(4)],
                  YH, sg1, 3, gate_bias)
            merged_split()
            for _ in range(4):
                next_hi()
            W.skip(8)

            norm(SEQ, real, lambda k: modc[:, 24 + k:25 + k])
            W.skip(1)
            act.wait_ge(ex_ready, 1)
            L.mark(af(rt[:, 0, :, :], rt[:, 0, :, :], ACT.Exp))
            af(rt[:, 15, :, 0:1], rt[:, 15, :, 0:1], ACT.Exp).then_inc(ex_done, 1)

            def spread_routing():
                evac(combT[0:16, :], src=lambda s: PS[0:16, s, 0, :])
                for e in range(N_EXP):
                    evac(comb[:, e, :])

            def swiglu(units, T, last=False, between=None):
                def gates(waits, between=None):
                    b = W.g
                    next_hi()
                    for m in range(2):
                        if waits:
                            W.wait_released(b - 10 + m)
                        s = W.arrive()
                        W.release(af(sv(sg[:, m, 0:T], T), ps(s, T), ACT.Silu))
                    if between is not None:
                        between()
                    next_hi()
                    W.skip(2)

                gates(False, between)
                g0, c0 = W.g, hi["c"]
                W.wait_released(g0 - 2)
                W.wait_released(g0 - 1)
                pairs = (units - 1) // 2 - last
                with act.Fori(0, pairs) as i:
                    W.g, W.more = g0, i * 6
                    hi["c"], hi["rounds"] = c0, i * 2
                    for _ in range(2):
                        gates(True)
                        next_hi()
                        W.skip(KT)
                W.g, W.more = g0 + 24 * pairs, 0
                hi["c"], hi["rounds"] = c0 + 6 * pairs, 0
                for n in range(2 * pairs, units):
                    if n + 1 < units:
                        gates(True)
                    next_hi()
                    W.skip(KT)

            swiglu(N_EXP, SEQ, between=spread_routing)
            norm(TALL, every, tiles=False)
            swiglu(FF_UNITS, TALL)
            norm(TALL, lambda k: yacc[:, k, 0:TALL], split=False)
            norm(TALL, every, tiles=False)
            for m in range(4):
                if m % 2 == 0:
                    next_hi()
                s = W.arrive()
                W.release(af(sv(pc[:, m, :], TALL), ps(s, TALL), ACT.Copy))
            s = W.arrive()
            W.release(af(fz[0:8, 0, :].rearrange("p (b n) -> p b n", b=2), PS[0:8, s, 0:2, 0:TALL // 2], ACT.Identity,
                         bias=b_fox[0:8, 0:1]))
            W.wait_released(W.g - 1)
            L(af(fz[0:8, 1, :], fz[0:8, 0, :], ACT.Abs))
            L(af(fz[0:8, 1, :], fz[0:8, 1, :], ACT.Exp, scale=-1.0))
            af(fz[0:8, 1, :], fz[0:8, 1, :], ACT.Ln, bias=eps[0:8, 1:2]).then_inc(gla_act, 1)
            for _ in range(2):
                next_hi()
                W.skip(2)
            for h in range(8):
                s = W.arrive()
                W.release(af(sv(Hf[:, h, :], TALL), ps(s, TALL), ACT.Copy))
            for _ in range(2):
                next_hi()
                W.skip(2)
            for m in range(4):
                if m % 2 == 0:
                    next_hi()
                s = W.arrive()
                W.release(af(sv(k2[:, m, :], TALL), ps(s, TALL), ACT.Copy))
            for m in range(4):
                if m % 2 == 0:
                    next_hi()
                evac(q2[:, m, :])
            for c0 in (0, 256):
                next_hi()
                for t in range(5):
                    n = P if t < 4 else META
                    evac(v2[0:n, t, c0:c0 + 256], src=lambda s: PS[0:n, s, 0, 0:256])
            combos2 = [(i, h) for i in range(NTOK) for h in range(8)]
            attention(combos2, lambda i: META + P * (i + 1), lg2, pr2, 0.125, pT2, True,
                      lambda i, h: ya2[64 * (h % 2):64 * (h % 2) + 64, h // 2, P * i:P * i + P],
                      lambda s, h: PS[64 * (h % 2):64 * (h % 2) + 64, s, 0, 0:P])
            n_["yl"] += 8
            merge([ya2[:, k, :] for k in range(4)] + [yc2[:, k, :] for k in range(4)], YH2, sg2, 2, None)
            merged_split()
            for _ in range(4):
                next_hi()
            W.skip(8)
            norm(SEQ, y_real, split=False)
            norm(SEQ, real, tiles=False)
            swiglu(FF_UNITS, SEQ, last=True)
            norm(SEQ, y_real, split=False)
            for t in range(NTOK):
                for half in range(2):
                    s = W.arrive()
                    ins = af(o_tok[:, t, 512 * half:512 * half + 512], ps(s), ACT.Copy)
                    W.release(ins)
                    W.wait_released(W.g - 1)
                    act.sem_inc(o_ready, 1)

        @block.vector
        def _(dve):
            W = PsumWalk(dve, ready, free)
            L = Link(dve, dve_link)
            v_ = nc.vector
            tt, ts, stt = v_.tensor_tensor, v_.tensor_scalar, v_.scalar_tensor_tensor
            n_ = {"r": 0, "hh": 0, "mod": 0, "hn": 0, "sq": 0, "p": 0, "y": 0}

            def ps(s, T=SEQ):
                return PS[:, s, 0, 0:T] if T <= 512 else PS[:, s, 0:2, 0:T // 2]

            def sv(ap, T):
                return ap if T <= 512 else ap.rearrange("p (b n) -> p b n", b=2)

            def h_lo(T):
                for k in range(KT):
                    n_["hh"] += 1
                    dve.wait_ge(hh_ready, n_["hh"])
                    tt(HL[:, k, 0:T], Hf[:, k, 0:T], HH[:, k, 0:T].bitcast(F32), ALU.subtract).then_inc(hl_ready, 1)

            def add_squares(sq, T):
                total = sq[:, SQ_OWN, 0:T]
                for k in range(SQ_OWN + 1, KT):
                    dve.wait_ge(sq_ready, n_["sq"] + k + 1)
                    ins = tt(total, total, sq[:, k, 0:T], ALU.add)
                    if k < KT - 1:
                        L(ins)
                    else:
                        ins.then_inc(sqsum_ready, 1)
                n_["sq"] += KT

            def norm(T, src, gain, post=None):
                G, J = token_groups(T)
                add_squares(Hf, T)
                W.wait_released(W.g)
                W.skip()
                v_.reciprocal(rsc[0:G, 0:J], rsc[0:G, 0:J]).then_inc(rs_ready, 1)
                apply_rms(T, src, gain, post)

            def apply_rms(T, src, gain, post=None):
                s = W.arrive()
                for k in range(KT):
                    ins = stt(sv(Hf[:, k, 0:T], T), sv(src(k), T), gain(k), ps(s, T), ALU.mult, ALU.mult)
                    if k == KT - 1:
                        W.release(ins)
                    elif post is None:
                        ins.then_inc(hraw_ready, 1)
                    else:
                        L.mark(ins)
                if post is not None:
                    L.wait()
                    W.wait_released(W.g - 1)
                    for k in range(KT):
                        n_["r"] += 1
                        tt(post(k), post(k), Hf[:, k, 0:T], ALU.add).then_inc(r_ready, 1)
                    dve.wait_ge(r_ready, n_["r"])
                else:
                    h_lo(T)

            def mod_products():
                n = n_["mod"]
                n_["mod"] += 1
                if n in MOD_PE:
                    return
                d = mod_dve(n)
                raw, landed, count = mod_slot(n)
                dve.wait_ge(landed, count)
                o = macc[:, d % 2, :]
                L(ts(o, raw[:, 0, :], c_act[:, 0:1], None, ALU.mult))
                for k in range(1, KT - 1):
                    L(stt(o, raw[:, k, :], c_act[:, k:k + 1], o, ALU.mult, ALU.add))
                stt(o, raw[:, KT - 1, :], c_act[:, KT - 1:KT], o, ALU.mult, ALU.add).then_inc(macc_ready, 1)
                dve.wait_ge(macc_ready, d + 1)
                dve.sem_inc(mod_used, 1)

            def mod_evac(n):
                s = W.arrive()
                W.release(tt(modc[:, 2 * n:2 * n + 2], PS[:, s, 0, 0:2], C1[:, 2 * n:2 * n + 2], ALU.add))

            W.skip(KT)
            s = W.arrive()
            W.release(v_.tensor_copy(C1[:, 0:V1_ROWS], PS[:, s, 0, 0:V1_ROWS]))
            W.wait_released(W.g - 1)
            dve.sem_inc(cols_ready, 1)
            s = W.arrive()
            W.release(v_.tensor_copy(C2[:, 0:V2_ROWS], PS[:, s, 0, 0:V2_ROWS]))
            W.skip(1)
            s = W.arrive()
            L.mark(v_.tensor_copy(dist_sb[0:4, 0:512], PS[0:4, s, 0, :]))
            W.release(v_.tensor_copy(dist_sb[0:4, 512:640], PS[0:4, s, 1, 0:128]))
            W.wait_released(W.g - 1)
            dve.sem_inc(dist_ready, 1)
            dve.wait_ge(consts, 8)
            L.mark(v_.tensor_copy(tri2[0:64, :], tri[0:64, 0:64]))
            L.mark(v_.tensor_copy(tri2[64:128, :], tri[64:128, 64:128]))
            qn = V1["dsa_qnorm_g"]
            L(ts(eps[:, 2:3], C1[:, qn:qn + 1], float(P) ** -0.5, None, ALU.mult))
            dve.wait_ge(cact_ready, 1)
            root1 = W.g
            W.skip(1)
            evacuated = 0
            own = [n for n in range(MOD1) if n not in MOD_PE]
            for x, n in enumerate(own):
                n_["mod"] = n
                if x >= 2:
                    while evacuated <= own[x - 2]:
                        mod_evac(evacuated)
                        evacuated += 1
                mod_products()
                if x == 0:
                    add_squares(squares1, SEQ)
            for m in range(evacuated, MOD1):
                mod_evac(m)
            W.wait_released(W.g - 1)

            def adaptive_gain(dst, sc0, g0):
                L(stt(dst[:, :], modc[:, sc0:sc0 + KT], 1.0, C1[:, g0:g0 + KT], ALU.add, ALU.mult))

            adaptive_gain(gain1, 8, V1["g_norm1"])
            W.wait_released(10)
            W.wait_released(root1)
            v_.reciprocal(rsc[:, 0:NTOK], rsc[:, 0:NTOK]).then_inc(rs_ready, 1)
            apply_rms(SEQ, lambda k: R[:, k, META:TALL], lambda k: gain1[:, k:k + 1])
            W.skip(3)

            L(ts(keep0[:, :], outside[:, :], 0.0, BIG, ALU.is_ge, ALU.mult))
            rounds = [(i, r) for i in (1, 2, 3) for r in range(TOPK // 8)]
            done_mods = MOD1
            v_tiles = []
            for n, (kind, _) in enumerate(P1):
                now = MODS_AT[n]
                for _ in range(now):
                    mod_products()
                if n == n_p1 - 1:
                    for g in v_tiles:
                        W.wait_released(g)
                    dve.wait_ge(gm_in, 64)
                    for t in range(NTOK):
                        L.mark(v_.bn_stats(stats[:, t, :], v[:, t, :]))
                    L.wait()
                    for t in range(NTOK):
                        ins = v_.bn_aggr(mv[:, t, :], stats[:, t, :])
                    ins.then_inc(var_ready, 1)
                    W.wait_released(W.g)
                    W.skip()
                    tt(wsT[:, :, :], wsT[:, :, :], tri[:, :].unsqueeze(1).to_broadcast([P, 4, P]), ALU.mult).then_inc(wsT_ready, 1)
                    dve.wait_ge(std_ready, 1)
                    dve.wait_ge(var_ready, 1)
                    L(v_.reciprocal(rstd[:, :], rstd[:, :]))
                    for t in range(NTOK):
                        L.mark(ts(v[:, t, :], v[:, t, :], mv[:, t, 0:1], rstd[:, t:t + 1], ALU.subtract, ALU.mult))
                    L.wait()
                    for t in range(NTOK):
                        L.mark(tt(v[:, t, :], v[:, t, :], ln_rows[:, 0, :], ALU.mult))
                    L.wait()
                    for t in range(NTOK):
                        ins = tt(v[:, t, :], v[:, t, :], ln_rows[:, 1, :], ALU.add)
                    ins.then_inc(gmv_ready, 1)
                W.skip(2 if kind == "fm" else NTOK)
                if n in (1, 2):
                    v_tiles += range(W.g - NTOK, W.g)
                if n == 0:
                    for x in range(12):
                        i, h = x // 4 + 1, x % 4
                        w = (i + 1) * P
                        W.wait_released(W.g)
                        W.skip()
                        src = relu_s[:, x % 2, 0:w]
                        col = iw[:, i, h:h + 1]
                        if h == 0:
                            ins = ts(sc[i][:, :], src, col, 0.0, ALU.mult, ALU.add)
                        else:
                            ins = stt(sc[i][:, :], src, col, sc[i][:, :], ALU.mult, ALU.add)
                        ins.then_inc(relu_used, 1)
                        dve.wait_ge(relu_used, x + 1)
                        if h == 3:
                            L(tt(sc[i][:, i * P:w], sc[i][:, i * P:w], outside[:, :], ALU.add))
                if n >= 1:
                    for i, r in rounds[4 * (n - 1):4 * n]:
                        L(v_.max(max8[:, :], sc[i][:, :]))
                        L(v_.match_replace(sc[i][:, :], max8[:, :], sc[i][:, :], REPLACED))
                        if r == TOPK // 8 - 1:
                            L(ts(sc[i][:, :], sc[i][:, :], REPLACED, BIG, ALU.is_equal, ALU.mult))
                for _ in range(now):
                    mod_evac(done_mods)
                    done_mods += 1

            W.wait_released(W.g - 1)
            for g in range(4):
                s = W.arrive()
                m = mixt[:, g % 2, :]
                W.release(tt(m.rearrange("p (t n) -> p t n", t=NTOK), PS[:, s, 0, :].rearrange("p (t n) -> p t n", t=NTOK),
                             bs_rows[:, g, :].unsqueeze(1).to_broadcast([P, NTOK, P]), ALU.add))
                W.wait_released(W.g - 1)
                ins = tt(u[:, g, :], u[:, g, :], m, ALU.mult)
                L.mark(ins)
            L.wait()
            dve.sem_inc(gmlp_done, 1)

            def head_norms(items):
                for x, (src, gain, before, after) in enumerate(items):
                    if before:
                        before()
                    tt(sqh[:, x, :], src, src, ALU.mult).then_inc(hsq_ready, 1)
                W.wait_released(W.g)
                W.skip()
                c = NTOK * len(items)
                v_.reciprocal(rsc[:, 0:c], rsc[:, 0:c]).then_inc(rs_ready, 1)
                for src, gain, before, after in items:
                    s = W.arrive()
                    W.release(stt(src, src, gain, ps(s), ALU.mult, ALU.mult))
                    if after:
                        W.wait_released(W.g - 1)
                        after()

            kn = V1["dsa_knorm_g"]
            head_norms([(dq[:, h, :], eps[:, 2:3], None, None) for h in range(4)] +
                       [(dk[:, h, :], C1[:, kn:kn + 1], None, None) for h in range(4)])

            def attention(combos, logits, pr, scale, width):
                N = len(combos)
                for n in range(N + 3):
                    if n < N:
                        i, h = combos[n]
                        c = n % 32
                        logits(n % 2, i, h, nmax[:, c:c + 1])
                        ts(nmax[:, c:c + 1], nmax[:, c:c + 1], -scale, None, ALU.mult).then_inc(lg_ready, 1)
                    if 0 <= n - 1 < N:
                        i, h = combos[n - 1]
                        c = (n - 1) % 32
                        n_["p"] += 1
                        dve.wait_ge(p_ready, n_["p"])
                        L(v_.reciprocal(rden[:, c:c + 1], den[:, c:c + 1]))
                        p = pr[:, (n - 1) % 3, 0:width(i)]
                        ts(p, p, rden[:, c:c + 1], None, ALU.mult).then_inc(pn_ready, 1)
                    if 0 <= n - 2 < N:
                        W.skip(1)
                    if 0 <= n - 3 < N:
                        W.skip(1)

            def dsa_logits(par, i, h, top):
                w = (i + 1) * P
                L(stt(bm[:, 0:w], keep[i][:, :], -BIG, bias_rev[:, h, 0:w][:, ::-1], ALU.add, ALU.add))
                s = W.arrive()
                W.release(v_.tensor_tensor_reduce(lg1[:, par, 0:w], PS[:, s, 0, 0:w], bm[:, 0:w], 1.0, -3.0e38, ALU.add, ALU.max, top))
                W.wait_released(W.g - 1)

            dve.wait_ge(bias_in, 64)
            combos1 = [(i, h) for i in range(NTOK) for h in range(4)]
            attention(combos1, dsa_logits, pr1, 1.0, lambda i: (i + 1) * P)

            def chunks(ap):
                return ap.rearrange("p (c t) -> p c t", t=CHUNK)

            for b in range(1, 5):
                W.wait_released(W.g - b)
            L(v_.memset(t2[:, :], 1.0))
            L(v_.memset(chunks(t2[:, :])[:, :, 0:1], 0.0))
            L.mark(v_.memset(Kp[:, :, :], 0.0))
            L.mark(v_.memset(Qp[:, :, :], 0.0))
            for j in range(2):
                W.skip(1)
                tj = (t0, t1)[j]
                dve.wait_ge(gla_act, j + 1)
                L(stt(tj[:, :], Bc[:, j, :], 0.0, tj[:, :], ALU.min, ALU.subtract))
                L(v_.tensor_tensor_scan(Bc[:, j, :], t2[:, :], tj[:, :], 0.0, ALU.mult, ALU.add))
            for j in range(2):
                L.mark(v_.tensor_copy(ebl[:, j, :], chunks(Bc[:, j, :])[:, :, CHUNK - 1:CHUNK].rearrange("p c t -> p (c t)")))
            L.wait()
            seq = 0
            tb = (t0, t1, t2)
            taken = []
            for j in range(2):
                Bj = Bc[:, j, :]
                for x in range(8):
                    if x < 7:
                        b = tb[(seq + x) % 3][:, :]
                        if seq + x >= 3:
                            L.wait(taken[seq + x - 3])
                        if x == 0:
                            ins = v_.tensor_copy(b, Bj)
                        elif x == 1:
                            ins = tt(chunks(b), chunks(Bj)[:, :, CHUNK - 1:CHUNK].to_broadcast([P, 8, CHUNK]), chunks(Bj), ALU.subtract)
                        elif x == 2:
                            subs = Bj.rearrange("p (c t) -> p c t", t=SUB)
                            ins = tt(b.rearrange("p (c t) -> p c t", t=SUB), subs[:, :, SUB // 2 - 1:SUB // 2].to_broadcast([P, SEQ // SUB, SUB]),
                                     subs, ALU.subtract)
                        else:
                            q = x - 3
                            pv = SUB * q + SUB // 2 - 1
                            ins = tt(chunks(b)[:, :, SUB * q:CHUNK], chunks(Bj)[:, :, SUB * q:CHUNK],
                                     chunks(Bj)[:, :, pv:pv + 1].to_broadcast([P, 8, CHUNK - SUB * q]), ALU.subtract)
                        ins.then_inc(exp_arg, 1)
                    if x >= 1:
                        y = x - 1
                        b = tb[(seq + y) % 3][:, :]
                        dve.wait_ge(gla_act, 2 + seq + y + 1)
                        if y == 0:
                            L.mark(stt(qe[:, j, :], gq[:, j, :], 0.125, b, ALU.mult, ALU.mult))
                        elif y == 1:
                            L.mark(tt(kk[:, j, :], gk[:, j, :], b, ALU.mult))
                        elif y == 2:
                            for q in range(4):
                                cs = slice(SUB * q, SUB * q + SUB)
                                L.mark(tt(chunks(Kp[:, q, :])[:, :, cs], chunks(gk[:, j, :])[:, :, cs], chunks(b)[:, :, cs], ALU.mult))
                        else:
                            q = y - 3
                            cs = slice(SUB * q, CHUNK)
                            L.mark(stt(chunks(Qp[:, q, :])[:, :, cs], chunks(gq[:, j, :])[:, :, cs], 0.125, chunks(b)[:, :, cs], ALU.mult, ALU.mult))
                        taken.append(L.n)
                seq += 7
                L.wait()
                dve.sem_inc(gla_dve, 1)
                for hh in range(2):
                    s = W.arrive()
                    W.release(tt(attT[:, 2 * j + hh, :, :], PS[:, s, 0, 0:256].rearrange("p (c t) -> p c t", t=CHUNK),
                                 tri2[:, :].unsqueeze(1).to_broadcast([P, NTOK, CHUNK]), ALU.mult))
                W.skip(1)
            W.wait_released(W.g - 2)
            dve.sem_inc(exp_arg, 1)
            dve.wait_ge(gla_act, 2 + seq + 1)
            for c in range(7):
                s = W.arrive()
                if c == 0:
                    ins = v_.tensor_copy(Sall[:, 1, :, :], PS[:, s, 0, 0:256].rearrange("p (j e) -> p j e", j=2))
                else:
                    L(stt(Sall[:, c + 1, 0, :], Sall[:, c, 0, :], ebl[:, 0, c:c + 1], PS[:, s, 0, 0:P], ALU.mult, ALU.add))
                    ins = stt(Sall[:, c + 1, 1, :], Sall[:, c, 1, :], ebl[:, 1, c:c + 1], PS[:, s, 0, P:2 * P], ALU.mult, ALU.add)
                W.release(ins)
                W.wait_released(W.g - 1)
            dve.sem_inc(gla_dve, 1)
            gn = V1["gla_norm_g"]
            g0 = W.g
            W.skip(4)
            head_norms([(og[:, h, :], C1[:, gn:gn + 1], (lambda g=g0 + h: W.wait_released(g)),
                         (lambda h=h: L.mark(tt(gr[:, h, :], gr[:, h, :], og[:, h, :], ALU.mult)))) for h in range(4)])
            L.wait()

            def merge(srcs, yh, yl, sg_, mt, n_br):
                dve.sem_inc(y_src, 1)
                for k in range(KT):
                    L.mark(v_.memset(Hf[:, k, 0:SEQ], 0.0))
                L.wait()
                for n, y in enumerate(srcs):
                    n_["y"] += 1
                    dve.wait_ge(yh_ready, n_["y"])
                    tt(yl[:, n, :], y, yh[:, n, :].bitcast(F32), ALU.subtract).then_inc(yl_ready, 1)
                for mq in range(2):
                    g0 = W.g

                    def body():
                        W.skip(4)
                        for m in range(4):
                            s = W.arrive()
                            W.wait_released(W.g - 4)
                            W.release(tt(mt[:, m % 2, :], ps(s), sg_[:, m, :], ALU.mult))
                            W.wait_released(W.g - 1)
                            h = Hf[:, 4 * mq + m, 0:SEQ]
                            L(tt(h, h, mt[:, m % 2, :], ALU.add))

                    body()
                    with dve.Fori(0, n_br - 1) as i:
                        W.g = g0 + 8
                        W.more, L.more = i * 2, i * 4
                        body()
                    W.g = g0 + 8 * n_br
                    W.more = L.more = 0
                    L.n += 4 * (n_br - 2)
                dve.sem_inc(merged_ready, 1)
                h_lo(SEQ)

            merge([u[:, k, :] for k in range(4)] + [gr[:, k, :] for k in range(4)] + [dq[:, k, :] for k in range(4)],
                  YH, YL, sg1, mt1, 3)
            for m in range(KT):
                s = W.arrive()
                W.release(stt(R[:, m, META:TALL], ps(s), modc[:, 16 + m:17 + m], R[:, m, META:TALL], ALU.mult, ALU.add))
            adaptive_gain(gain2, 32, V1["g_norm2"])
            W.wait_released(W.g - 1)
            W.wait_released(W.g - 2)
            W.wait_released(W.g - 3)
            W.wait_released(W.g - 4)
            norm(SEQ, lambda k: R[:, k, META:TALL], lambda k: gain2[:, k:k + 1])

            s = W.arrive()
            W.release(tt(rl[:, :, :], PS[:, s, 0, 0:80].rearrange("p (t c) -> p t c", c=20),
                         b_route[:, 0:20].unsqueeze(1).to_broadcast([P, NTOK, 20]), ALU.add))
            W.wait_released(W.g - 1)

            def r(n, a_=0, b_=4):
                return rt[:, n, :, a_:b_]

            def bc(ap):
                return ap.to_broadcast([P, NTOK, 4])

            def first_of(dst, eq, seen):
                L(v_.tensor_copy(r(dst, 0, 1), r(eq, 0, 1)))
                L(v_.tensor_copy(r(seen, 0, 1), r(eq, 0, 1)))
                for c in range(1, 4):
                    L(ts(r(dst, c, c + 1), r(seen, c - 1, c), -1.0, 1.0, ALU.mult, ALU.add))
                    L(tt(r(dst, c, c + 1), r(dst, c, c + 1), r(eq, c, c + 1), ALU.mult))
                    L(tt(r(seen, c, c + 1), r(seen, c - 1, c), r(dst, c, c + 1), ALU.add))

            gl = rl[:, :, 0:4]
            L(v_.tensor_reduce(r(1, 0, 1), gl, AX, ALU.max))
            L(tt(r(2), gl, bc(r(1, 0, 1)), ALU.is_equal))
            first_of(3, 2, 4)
            L(tt(r(0), gl, bc(r(1, 0, 1)), ALU.subtract))
            L(tt(r(5), rl[:, :, 4:8], bc(r(3, 0, 1)), ALU.mult))
            for gi in range(1, 4):
                L(tt(r(6), rl[:, :, 4 + 4 * gi:8 + 4 * gi], bc(r(3, gi, gi + 1)), ALU.mult))
                L(tt(r(5), r(5), r(6), ALU.add))
            L(v_.tensor_reduce(r(7, 0, 1), r(5), AX, ALU.max))
            L(tt(r(2), r(5), bc(r(7, 0, 1)), ALU.is_equal))
            first_of(8, 2, 4)
            L(stt(r(9), r(8), -BIG, r(5), ALU.mult, ALU.add))
            L(v_.tensor_reduce(r(7, 1, 2), r(9), AX, ALU.max))
            L(tt(r(2), r(9), bc(r(7, 1, 2)), ALU.is_equal))
            first_of(10, 2, 4)
            L(tt(r(15, 0, 1), r(7, 1, 2), r(7, 0, 1), ALU.subtract))
            dve.sem_inc(ex_ready, 1)
            dve.wait_ge(ex_done, 1)
            L(v_.tensor_reduce(r(11, 0, 1), r(0), AX, ALU.add))
            L(v_.reciprocal(r(11, 1, 2), r(11, 0, 1)))
            L(ts(r(12, 0, 1), r(15, 0, 1), 1.0, None, ALU.add))
            L(v_.reciprocal(r(12, 1, 2), r(12, 0, 1)))
            L(tt(r(12, 2, 3), r(12, 1, 2), r(11, 1, 2), ALU.mult))
            L(tt(r(12, 3, 4), r(12, 2, 3), r(15, 0, 1), ALU.mult))
            L(tt(r(13), r(8), bc(r(12, 2, 3)), ALU.mult))
            L(tt(r(14), r(10), bc(r(12, 3, 4)), ALU.mult))
            L(tt(r(13), r(13), r(14), ALU.add))
            for gi in range(4):
                L(tt(rc[:, :, 4 * gi:4 * gi + 4], r(13), bc(r(3, gi, gi + 1)), ALU.mult))
            dve.sem_inc(router_done, 1)
            gate1 = W.g
            W.skip(2)
            W.wait_made(W.g)
            W.skip(1)
            W.skip(N_EXP)

            units_done = {"n": 0}

            def swiglu(units, T, weight=None, first_gate=None):
                for k in range(KT):
                    L.mark(v_.memset(yacc[:, k, 0:T], 0.0))
                L.wait()
                base = units_done["n"]

                def up(n, par, more=0, gate=None):
                    if gate is None:
                        W.skip(2)
                    for m in range(2):
                        s = W.arrive()
                        W.wait_released(W.g - 2 if gate is None else gate + m)
                        f = actf[:, m, 0:T]
                        W.release(tt(sv(f, T), ps(s, T), sv(sg[:, m, 0:T], T), ALU.mult))
                        W.wait_released(W.g - 1)
                        if weight is not None:
                            L(tt(f, f, weight(n), ALU.mult))
                        L(v_.tensor_copy(ah[:, par, m, 0:T], f))
                        ins = tt(al[:, par, m, 0:T], f, ah[:, par, m, 0:T].bitcast(F32), ALU.subtract)
                        if m == 1:
                            ins.then_inc(moe_act, 1)

                def down():
                    for m in range(KT):
                        s = W.arrive()
                        y = sv(yacc[:, m, 0:T], T)
                        W.release(tt(y, y, ps(s, T), ALU.add))

                up(0, 0, gate=first_gate)
                pairs = (units - 1) // 2
                g0, l0 = W.g, L.n
                per = 4 if weight is None else 8
                with dve.Fori(0, pairs) as i:
                    W.g, L.n = g0, l0
                    W.more, L.more = i * 6, i * per
                    for par in range(2):
                        up(i * 2 + (par + 1), 1 - par, i * 2)
                        down()
                W.g, L.n = g0 + 24 * pairs, l0 + per * pairs
                W.more = L.more = 0
                for n in range(2 * pairs, units):
                    if n + 1 < units:
                        up(n + 1, (n + 1) % 2)
                    down()
                units_done["n"] += units
                for b in range(1, 5):
                    W.wait_released(W.g - b)

            def routing(n):
                if isinstance(n, int):
                    return comb[:, n, :]
                return comb[:, bass.ds(n, 1), :].rearrange("p a n -> p (a n)")

            for b in range(1, 5):
                W.wait_released(W.g - b)
            swiglu(N_EXP, SEQ, routing, gate1)
            for m in range(KT):
                n_["r"] += 1
                stt(R[:, m, META:TALL], yacc[:, m, 0:SEQ], modc[:, 40 + m:41 + m], R[:, m, META:TALL], ALU.mult, ALU.add).then_inc(r_ready, 1)
            dve.wait_ge(r_ready, n_["r"])

            def c2(n):
                return lambda k: C2[:, 8 * n + k:8 * n + k + 1]

            L.mark(ts(gain1[:, :], C2[:, 8:16], 0.5, None, ALU.mult))
            L.mark(ts(gain2[:, :], C2[:, 40:48], 0.5, None, ALU.mult))
            L.wait()
            every = lambda k: R[:, k, 0:TALL]
            real = lambda k: R[:, k, META:TALL]
            norm(TALL, every, c2(0))
            swiglu(FF_UNITS, TALL)
            norm(TALL, lambda k: yacc[:, k, 0:TALL], lambda k: gain1[:, k:k + 1], post=every)
            norm(TALL, every, c2(2))
            W.skip(4)
            W.skip(1)
            dve.wait_ge(gla_act, 2 + seq + 1 + 1)
            L(stt(fz[0:8, 1, :], fz[0:8, 0, :], 0.0, fz[0:8, 1, :], ALU.min, ALU.subtract))
            L(v_.memset(fz[0:8, 0, :], 1.0))
            L(v_.tensor_tensor_scan(negF[0:8, :], fz[0:8, 0, :], fz[0:8, 1, :], 0.0, ALU.mult, ALU.subtract))
            L(ts(negF[0:8, :], negF[0:8, :], float(8), None, ALU.mult))
            dve.sem_inc(negF_ready, 1)
            for m in range(4):
                s = W.arrive()
                W.wait_released(W.g - 5)
                W.release(tt(sv(pc[:, m, :], TALL), ps(s, TALL), sv(pc[:, m, :], TALL), ALU.mult))
                W.wait_released(W.g - 1)
                for j in range(3):
                    src, w = pc[:, m, META - 2 + j:META - 2 + j + SEQ], C2[:, CONV_ROW + 4 * j + m:CONV_ROW + 4 * j + m + 1]
                    if j == 0:
                        L(ts(yc2[:, m, :], src, w, None, ALU.mult))
                    else:
                        L(stt(yc2[:, m, :], src, w, yc2[:, m, :], ALU.mult, ALU.add))
            f0 = W.g
            W.skip(8)
            for m in range(4):
                s = W.arrive()
                W.release(tt(yc2[:, m, :], ps(s), yc2[:, m, :], ALU.mult))
            W.skip(4 + 4 + 10)

            def fox_logits(par, i, h, top):
                s = W.arrive()
                row = lg2[:, par, :]
                d0 = META + P * i
                n0 = min(512, d0 + P)
                if d0 + P > n0:
                    L.mark(tt(row[:, 512:TALL], PS[:, s, 1, 0:TALL - 512], Hf[:, h, 512:TALL], ALU.add))
                W.release(tt(row[:, 0:n0], PS[:, s, 0, 0:n0], Hf[:, h, 0:n0], ALU.add))
                W.wait_released(W.g - 1)
                L(tt(row[:, d0:d0 + P], row[:, d0:d0 + P], outside[:, :], ALU.add))
                L(v_.tensor_reduce(top, row[:, 0:d0 + P], AX, ALU.max))

            for b in range(1, 9):
                W.wait_released(f0 + 8 - b)
            combos2 = [(i, h) for i in range(NTOK) for h in range(8)]
            attention(combos2, fox_logits, pr2, 0.125, lambda i: META + P * (i + 1))
            W.wait_released(W.g - 1)
            merge([ya2[:, k, :] for k in range(4)] + [yc2[:, k, :] for k in range(4)], YH2, YL2, sg2, mt2, 2)
            for m in range(KT):
                s = W.arrive()
                W.release(v_.tensor_copy(yacc[:, m, 0:SEQ], ps(s)))
            for b in range(1, 5):
                W.wait_released(W.g - b)
            norm(SEQ, lambda k: yacc[:, k, 0:SEQ], c2(3), post=real)
            norm(SEQ, real, c2(4))
            swiglu(FF_UNITS, SEQ)
            norm(SEQ, lambda k: yacc[:, k, 0:SEQ], lambda k: gain2[:, k:k + 1], post=real)
            dve.sem_inc(r_done, 1)


_OUT = (1, SEQ, D)
_INS = ["x", "c", "w_mod", "b_mod", "g_norm1", "g_norm2", "w_in", "gmlp_ln_g", "gmlp_ln_b", "gmlp_w_s", "gmlp_b_s",
        "gla_w_gate2", "gla_b_gate", "gla_norm_g", "dsa_qnorm_g", "dsa_knorm_g", "rel_bias", "w_branch",
        "b_branch_gate", "w_out", "w_group", "b_group", "w_router", "b_router", "w_exp_gate", "w_exp_up",
        "w_exp_down", "meta_tokens_2", "w_in_2", "b_forget_2", "conv_w_2", "w_attn_branch_2", "w_conv_branch_2",
        "w_out_2", "g_ffn1_pre_2", "g_ffn1_post_2", "w_ffn1_in_2", "w_ffn1_out_2", "g_mix_pre_2", "g_mix_post_2",
        "g_ffn2_pre_2", "g_ffn2_post_2", "w_ffn2_in_2", "w_ffn2_out_2"]


def kernel(**inputs):
    import numpy as _np
    import concourse.bacc as _bacc
    from concourse import mybir as _mybir
    from concourse.bass_utils import run_bass_kernel_spmd as _run

    nc = _bacc.Bacc("TRN2", target_bir_lowering=False, num_devices=1, dynamic_dma_scratch_size=1024)
    arrays, args = {}, {}
    for name in _INS:
        x = _np.ascontiguousarray(inputs[name])
        arrays[f"in_{name}"] = x
        args[name] = nc.dram_tensor(f"in_{name}", x.shape, _mybir.dt.from_np(x.dtype), kind="ExternalInput").ap()
    arrays["one_hot"] = distance_buckets()
    one_hot = nc.dram_tensor("one_hot", (32, 640), _mybir.dt.float32, kind="ExternalInput").ap()
    out = nc.dram_tensor("out_0", _OUT, _mybir.dt.float32, kind="ExternalOutput").ap()
    build(nc, args, one_hot, out)
    r = _run(nc, [arrays], core_ids=[0])
    return r.results[0]["out_0"]
```
